# Optimizing a Trainium2 kernel written in Bass

```python
import math
import jax, jax.numpy as jnp
from jax import lax
import numpy as np

D_MODEL = 1024
BATCH = 1
SEQ = 256
DEPTH = 1

N_META = 16
BLOCK = 128
PREFIX = BLOCK
N_PAD = PREFIX - N_META
ATT_HEADS = 16
ATT_KV_HEADS = 2
ATT_GROUP = ATT_HEADS // ATT_KV_HEADS
ATT_HEAD_DIM = 64
WINDOW = 128
RET_HEADS = 4
RET_KEY_DIM = 128
RET_VALUE_DIM = 256
ATT_Q_W = ATT_HEADS * ATT_HEAD_DIM
ATT_KV_W = ATT_KV_HEADS * ATT_HEAD_DIM
RET_QK_W = RET_HEADS * RET_KEY_DIM
RET_V_W = RET_HEADS * RET_VALUE_DIM
GATE_W = 2 * D_MODEL
SPLIT_POINTS = (ATT_Q_W,
                ATT_Q_W + ATT_KV_W,
                ATT_Q_W + 2 * ATT_KV_W,
                ATT_Q_W + 2 * ATT_KV_W + RET_QK_W,
                ATT_Q_W + 2 * ATT_KV_W + 2 * RET_QK_W,
                ATT_Q_W + 2 * ATT_KV_W + 2 * RET_QK_W + RET_V_W,
                ATT_Q_W + 2 * ATT_KV_W + 2 * RET_QK_W + 2 * RET_V_W)
IN_WIDTH = ATT_Q_W + 2 * ATT_KV_W + 2 * RET_QK_W + 2 * RET_V_W + GATE_W
N_EXPERTS = 32
TOP_K = 4
D_FF = 1024
SWIGLU_ALPHA = 1.702
SWIGLU_LIMIT = 7.0
MOE_BLOCK = 256
EPS = 1e-5

kernel_name = "hybrid_swa_retention_moe_meta"

def rms_norm(x, gain=None):
    xf = x.astype(jnp.float32)
    y = xf * lax.rsqrt(jnp.mean(xf * xf, axis=-1, keepdims=True) + EPS)
    if gain is not None:
        y = y * gain.astype(jnp.float32)
    return y.astype(x.dtype)

def alibi_slopes(n_heads):
    return 2.0 ** (-8.0 * jnp.arange(1, n_heads + 1, dtype=jnp.float32) / n_heads)

def sliding_window_attention(q, k, v, sinks):
    b, l = q.shape[:2]
    nb = l // BLOCK
    qb = q.reshape(b, nb, BLOCK, ATT_KV_HEADS, ATT_GROUP, ATT_HEAD_DIM)
    kb = k.reshape(b, nb, BLOCK, ATT_KV_HEADS, ATT_HEAD_DIM)
    vb = v.reshape(b, nb, BLOCK, ATT_KV_HEADS, ATT_HEAD_DIM)
    pad_prev = ((0, 0), (1, 0), (0, 0), (0, 0), (0, 0))
    k_band = jnp.concatenate([jnp.pad(kb[:, :-1], pad_prev), kb], axis=2)
    v_band = jnp.concatenate([jnp.pad(vb[:, :-1], pad_prev), vb], axis=2)
    k_meta = k[:, N_PAD:PREFIX]
    v_meta = v[:, N_PAD:PREFIX]
    meta_pos = jnp.arange(N_PAD, PREFIX)
    q_pos = jnp.arange(l).reshape(nb, BLOCK)
    slopes = alibi_slopes(ATT_HEADS).reshape(ATT_KV_HEADS, ATT_GROUP)
    sink = sinks.astype(jnp.float32).reshape(ATT_KV_HEADS, ATT_GROUP)
    scale = ATT_HEAD_DIM ** -0.5

    def one_block(args):
        q_blk, kb_blk, vb_blk, qp = args
        kp = jnp.concatenate([qp - BLOCK, qp])
        d_band = qp[:, None] - kp[None, :]
        ok_band = (d_band >= 0) & (d_band < WINDOW) & (kp[None, :] >= PREFIX)
        d_meta = qp[:, None] - meta_pos[None, :]
        ok_meta = d_meta >= 0
        dist = jnp.abs(jnp.concatenate([d_meta, d_band], axis=1)).astype(jnp.float32)
        ok = jnp.concatenate([ok_meta, ok_band], axis=1)
        keys = jnp.concatenate([k_meta, kb_blk], axis=1)
        vals = jnp.concatenate([v_meta, vb_blk], axis=1)
        s = jnp.einsum('bqhgd,bkhd->bhgqk', q_blk, keys).astype(jnp.float32) * scale
        s = s - slopes[:, :, None, None] * dist
        s = jnp.where(ok, s, -jnp.inf)
        sink_col = jnp.broadcast_to(sink[None, :, :, None, None], s.shape[:-1] + (1,))
        p = jax.nn.softmax(jnp.concatenate([s, sink_col], axis=-1), axis=-1)[..., :-1]
        return jnp.einsum('bhgqk,bkhd->bqhgd', p.astype(vals.dtype), vals)

    out = lax.map(one_block, (jnp.moveaxis(qb, 1, 0), jnp.moveaxis(k_band, 1, 0),
                              jnp.moveaxis(v_band, 1, 0), q_pos))
    return jnp.moveaxis(out, 0, 1).reshape(b, l, ATT_Q_W)

def chunkwise_retention(q, k, v):
    out_dtype = q.dtype
    q, k, v = (a.astype(jnp.float32) for a in (q, k, v))
    b, l = q.shape[:2]
    nc = l // BLOCK
    log_g = jnp.log1p(-(2.0 ** (-5.0 - jnp.arange(RET_HEADS, dtype=jnp.float32))))
    idx = jnp.arange(BLOCK, dtype=jnp.float32)
    diff = idx[:, None] - idx[None, :]
    decay_intra = jnp.where(diff >= 0, jnp.exp(log_g[:, None, None] * jnp.maximum(diff, 0.0)), 0.0)
    decay_in = jnp.exp(log_g[None, :] * (idx[:, None] + 1.0))
    decay_out = jnp.exp(log_g[None, :] * (BLOCK - 1.0 - idx[:, None]))
    decay_chunk = jnp.exp(log_g * BLOCK)
    qc = q.reshape(b, nc, BLOCK, RET_HEADS, RET_KEY_DIM)
    kc = k.reshape(b, nc, BLOCK, RET_HEADS, RET_KEY_DIM)
    vc = v.reshape(b, nc, BLOCK, RET_HEADS, RET_VALUE_DIM)
    s = jnp.einsum('bnqhd,bnkhd->bnhqk', qc, kc) * decay_intra
    intra = jnp.einsum('bnhqk,bnkhe->bnqhe', s, vc)
    kv = jnp.einsum('bnkhd,bnkhe->bnhde', kc * decay_out[None, None, :, :, None], vc)

    def step(state, kv_n):
        return state * decay_chunk[:, None, None] + kv_n, state

    init = jnp.zeros((b, RET_HEADS, RET_KEY_DIM, RET_VALUE_DIM), jnp.float32)
    _, prev = lax.scan(step, init, jnp.moveaxis(kv, 1, 0))
    prev = jnp.moveaxis(prev, 0, 1)
    cross = jnp.einsum('bnqhd,bnhde->bnqhe', qc, prev) * decay_in[None, None, :, :, None]
    return (intra + cross).reshape(b, l, RET_HEADS, RET_VALUE_DIM).astype(out_dtype)

def moe_ffn(u, w_router, b_router, w_gate_up, b_gate_up, w_down, b_down):
    shape = u.shape
    t = u.reshape(-1, D_MODEL)
    n = t.shape[0]
    logits = (t @ w_router + b_router).astype(jnp.float32)
    top_logit, top_idx = lax.top_k(logits, TOP_K)
    top_w = jax.nn.softmax(top_logit, axis=-1)
    e_flat = top_idx.reshape(-1)
    tok_flat = jnp.repeat(jnp.arange(n, dtype=jnp.int32), TOP_K)
    w_flat = top_w.reshape(-1)
    order = jnp.argsort(e_flat)
    e_sorted = e_flat[order]
    counts = jnp.bincount(e_flat, length=N_EXPERTS)
    padded = (counts + MOE_BLOCK - 1) // MOE_BLOCK * MOE_BLOCK
    start = jnp.cumsum(counts) - counts
    pend = jnp.cumsum(padded)
    pstart = pend - padded
    dest = pstart[e_sorted] + jnp.arange(n * TOP_K) - start[e_sorted]
    n_rows = (-(-(n * TOP_K) // MOE_BLOCK) + N_EXPERTS) * MOE_BLOCK
    n_blocks = n_rows // MOE_BLOCK
    row_tok = jnp.full((n_rows,), n, jnp.int32).at[dest].set(tok_flat[order])
    row_w = jnp.zeros((n_rows,), jnp.float32).at[dest].set(w_flat[order])
    block_expert = jnp.minimum(
        jnp.searchsorted(pend, jnp.arange(n_blocks) * MOE_BLOCK, side='right'), N_EXPERTS - 1)
    t_pad = jnp.concatenate([t, jnp.zeros((1, D_MODEL), t.dtype)], axis=0)

    def expert_block(args):
        rows, e = args
        xb = t_pad[rows]
        gu = xb @ w_gate_up[e] + b_gate_up[e]
        gate, up = jnp.split(gu, 2, axis=-1)
        gate = jnp.minimum(gate, SWIGLU_LIMIT)
        up = jnp.clip(up, -SWIGLU_LIMIT, SWIGLU_LIMIT)
        act = (up + 1.0) * gate * jax.nn.sigmoid(SWIGLU_ALPHA * gate)
        return act @ w_down[e] + b_down[e]

    out = lax.map(expert_block, (row_tok.reshape(n_blocks, MOE_BLOCK), block_expert))
    out = out.reshape(n_rows, D_MODEL) * row_w[:, None].astype(out.dtype)
    y = jnp.zeros((n + 1, D_MODEL), out.dtype).at[row_tok].add(out)[:n]
    return y.reshape(shape)

def setup_inputs(seed: int = 0) -> dict:
    key = jax.random.key(seed)
    ks = jax.random.split(key, 20)
    f32 = jnp.float32
    nrm = lambda k, s, sc: jax.random.normal(k, s, f32) * sc
    return {
        "x": nrm(ks[0], (BATCH, SEQ, D_MODEL), 1.0),
        "meta_tokens": nrm(ks[1], (N_META, D_MODEL), 1.0),
        "mix_norm_gain": 1.0 + nrm(ks[2], (DEPTH, D_MODEL), 0.02),
        "w_in": nrm(ks[3], (DEPTH, D_MODEL, IN_WIDTH), D_MODEL ** -0.5),
        "q_norm_gain": 1.0 + nrm(ks[4], (DEPTH, ATT_HEAD_DIM), 0.02),
        "k_norm_gain": 1.0 + nrm(ks[5], (DEPTH, ATT_HEAD_DIM), 0.02),
        "attn_sinks": nrm(ks[6], (DEPTH, ATT_HEADS), 0.5),
        "w_attn_branch": nrm(ks[7], (DEPTH, ATT_Q_W, D_MODEL), ATT_Q_W ** -0.5),
        "w_ret_branch": nrm(ks[8], (DEPTH, RET_V_W, D_MODEL), RET_V_W ** -0.5),
        "w_out": nrm(ks[9], (DEPTH, D_MODEL, D_MODEL), D_MODEL ** -0.5),
        "ffn_norm_gain": 1.0 + nrm(ks[10], (DEPTH, D_MODEL), 0.02),
        "w_router": nrm(ks[11], (DEPTH, D_MODEL, N_EXPERTS), D_MODEL ** -0.5),
        "b_router": nrm(ks[12], (DEPTH, N_EXPERTS), 0.01),
        "w_gate_up": nrm(ks[13], (DEPTH, N_EXPERTS, D_MODEL, 2 * D_FF), D_MODEL ** -0.5),
        "b_gate_up": nrm(ks[14], (DEPTH, N_EXPERTS, 2 * D_FF), 0.01),
        "w_down": nrm(ks[15], (DEPTH, N_EXPERTS, D_FF, D_MODEL), D_FF ** -0.5),
        "b_down": nrm(ks[16], (DEPTH, N_EXPERTS, D_MODEL), 0.01),
    }

def reference(x, meta_tokens, mix_norm_gain, w_in, q_norm_gain, k_norm_gain, attn_sinks,
              w_attn_branch, w_ret_branch, w_out, ffn_norm_gain, w_router, b_router,
              w_gate_up, b_gate_up, w_down, b_down):
    b = x.shape[0]
    h = jnp.concatenate([
        jnp.zeros((b, N_PAD, D_MODEL), x.dtype),
        jnp.broadcast_to(meta_tokens.astype(x.dtype)[None], (b, N_META, D_MODEL)),
        x], axis=1)
    l = h.shape[1]
    occupied = (jnp.arange(l) >= N_PAD)[None, :, None, None]
    for layer in range(DEPTH):
        u = rms_norm(h, mix_norm_gain[layer])
        proj = u @ w_in[layer]
        aq, ak, av, rq, rk, rv, rg, gates = jnp.split(proj, SPLIT_POINTS, axis=-1)
        aq = rms_norm(aq.reshape(b, l, ATT_HEADS, ATT_HEAD_DIM), q_norm_gain[layer])
        ak = rms_norm(ak.reshape(b, l, ATT_KV_HEADS, ATT_HEAD_DIM), k_norm_gain[layer])
        av = av.reshape(b, l, ATT_KV_HEADS, ATT_HEAD_DIM)
        y_att = sliding_window_attention(aq, ak, av, attn_sinks[layer])
        rq = rq.reshape(b, l, RET_HEADS, RET_KEY_DIM)
        rk = jnp.where(occupied, rk.reshape(b, l, RET_HEADS, RET_KEY_DIM), 0.0).astype(rq.dtype) * (RET_KEY_DIM ** -0.5)
        rv = rv.reshape(b, l, RET_HEADS, RET_VALUE_DIM)
        y_ret = rms_norm(chunkwise_retention(rq, rk, rv)).reshape(b, l, RET_V_W) * jax.nn.silu(rg)
        g_att, g_ret = jnp.split(jax.nn.sigmoid(gates), 2, axis=-1)
        merged = g_att * (y_att @ w_attn_branch[layer]) + g_ret * (y_ret @ w_ret_branch[layer])
        h = h + merged @ w_out[layer]
        if layer == DEPTH - 1:
            h = h[:, PREFIX:]
        h = h + moe_ffn(rms_norm(h, ffn_norm_gain[layer]), w_router[layer], b_router[layer],
                        w_gate_up[layer], b_gate_up[layer], w_down[layer], b_down[layer])
    return h


_drawn_inputs = setup_inputs


def setup_inputs(seed=0):
    import zlib

    import numpy as np

    out = dict(_drawn_inputs(seed))
    spreads = {}
    factors = {'q_norm_gain': 6.981,
     'k_norm_gain': 4.021,
     'b_router': 3.115,
     'b_gate_up': 8.0,
     'b_down': 8.0}
    for name, (base, spread) in spreads.items():
        noise = np.random.default_rng([zlib.crc32(name.encode()), seed]).standard_normal(out[name].shape)
        drawn = base * np.exp(spread * noise) if base else spread * noise
        out[name] = __import__('jax').numpy.asarray(drawn.astype(out[name].dtype))
    for name, factor in factors.items():
        out[name] = (out[name] * factor).astype(out[name].dtype)
    return out
```

```python
from contextlib import ExitStack

import numpy as np

import concourse.bass as bass
from concourse import mybir

F32 = mybir.dt.float32
I32 = mybir.dt.int32
U32 = mybir.dt.uint32
ALU = mybir.AluOpType
ACT = mybir.ActivationFunctionType
AX = mybir.AxisListType

P = 128
D = 1024
KC = D // P
META, TOK = 16, 256
ALL = META + TOK
BLK = 128
HEADS, DH = 16, 64
PAIRS = HEADS // 2
RH, RDK, RDV = 4, 128, 256
EXPERTS, TOPK, FF = 32, 4, 1024
EPS = 1e-5
ALPHA, LIMIT = 1.702, 7.0
SLOTS = 12
UCOL = 256
CAP = 64
B1K, B2K = META + BLK, META + 2 * BLK
SCW = B1K + B2K
MASKED = -1.0e30

UNITS = (["kv"] + ["q"] * 4 + ["rq"] * 2 + ["rk"] * 2 + ["rg"] * 4 + ["ga"] * 2 + ["rv"] * 4
         + ["wa"] * 2 + ["ga", "wa"] * 2 + ["gr", "wr"] * 4 + ["out"] * 4)
NU = len(UNITS)


def chunk_table():
    seen, table = {}, []
    for u in UNITS:
        for half in range(2):
            kind = ("k", "v")[half] if u == "kv" else u
            n = seen.get(kind, 0)
            table.append((kind, n))
            seen[kind] = n + 1
    return table


CHUNKS = chunk_table()
AT = {c: i for i, c in enumerate(CHUNKS)}

CONST_COLS = {}


def _const_layout():
    at = 0
    for name, n in (("ones", P), ("ident", P), ("heads2", P), ("halves", 2), ("eps", 1), ("eps64", 1), ("slopes", 2 * HEADS),
                    ("tri", P), ("iota", TOK), ("alibi", SCW), ("decay", RH * TOK), ("decay_meta", RH * TOK)):
        CONST_COLS[name] = (at, n)
        at += n
    return at


N_CONST = _const_layout()
N_CONST_EARLY = CONST_COLS["tri"][0]

PARAM_COLS = {}


def _param_layout():
    at = 0
    for name, n in (("mix_gain", KC), ("ffn_gain", KC), ("q_gain", 1), ("k_gain", 1), ("sinks", HEADS),
                    ("b_router", EXPERTS), ("w_router", KC * EXPERTS), ("b_gate_up", EXPERTS * 16)):
        PARAM_COLS[name] = (at, n)
        at += n
    return at


N_PARAM = _param_layout()


def constants():
    t = np.zeros((P, N_CONST), np.float64)

    def put(name, a):
        at, n = CONST_COLS[name]
        t[:a.shape[0], at:at + n] = a.reshape(a.shape[0], n)

    p = np.arange(P)
    put("ones", np.ones((P, P)))
    put("ident", np.eye(P))
    put("heads2", (p[:, None] // DH == p[None, :] // DH) * 1.0)
    put("halves", (p[:, None] // DH == np.arange(2)[None]) * 1.0)
    put("eps", np.full((P, 1), EPS))
    put("eps64", np.full((P, 1), DH * EPS))
    slope = 2.0 ** (-8.0 * np.arange(1, HEADS + 1) / HEADS)
    by_pair = np.stack([slope[:PAIRS], slope[PAIRS:]], 1)
    put("slopes", np.broadcast_to(by_pair[None, None], (P, 2, PAIRS, 2)))
    put("tri", (p[:, None] < p[None, :]) * 1.0)
    put("iota", np.broadcast_to(np.arange(TOK)[None], (P, TOK)))
    near = np.where(p[:, None] >= p[None, :], -(p[:, None] - p[None, :]), MASKED)
    far = np.where(p[None, :] > p[:, None], -(BLK + p[:, None] - p[None, :]), MASKED)
    m = np.arange(META)[None]
    put("alibi", np.concatenate([-(META + p[:, None] - m), near, -(META + BLK + p[:, None] - m), far, near], 1))
    gamma = 1.0 - 2.0 ** (-5.0 - np.arange(RH))
    q = np.arange(TOK)
    scale = RDK ** -0.5
    d1 = q[None, :] - p[:, None]
    put("decay", np.where(d1[:, None] >= 0, gamma[None, :, None] ** np.maximum(d1, 0)[:, None], 0.0) * scale)
    dm = META + q[None, :] - np.arange(META)[:, None]
    put("decay_meta", gamma[None, :, None] ** dm[:, None] * scale)
    return t.astype(np.float32)


def build(nc, xT, mix_w, consts, params, b_down, w_gate_up, w_down, out):
    with ExitStack() as ctx:
        def sem(name):
            return ctx.enter_context(nc.semaphore(name))

        ring = ctx.enter_context(nc.sbuf_tensor("ring", [P, SLOTS, 2048], F32))
        arena_bytes = 113280
        arena = ctx.enter_context(nc.sbuf_tensor("arena", [P, arena_bytes // 4], F32))
        cursor = [0]

        def region(cols):
            at = cursor[0]
            cursor[0] += cols
            assert cursor[0] * 4 <= arena_bytes, (cursor[0] * 4, arena_bytes)
            return arena[:, at:at + cols]

        def cut(reg, at, shape, parts=P):
            n = int(np.prod(shape))
            v = reg[0:parts, at:at + n]
            if len(shape) == 2:
                return v.rearrange("p (a b) -> p a b", b=shape[1])
            if len(shape) == 3:
                return v.rearrange("p (a b c) -> p a b c", b=shape[1], c=shape[2])
            return v

        x_sb = cut(region(KC * ALL), 0, (KC, ALL))
        r_u = region(KC * ALL)
        u_sb, u2T = cut(r_u, 0, (KC, ALL)), cut(r_u, 0, (KC, TOK))
        r_q = region(KC * TOK)
        qT, sig_rg, merged = (cut(r_q, 0, (KC, TOK)) for _ in range(3))
        u2tok = cut(r_q, 0, (2, D))
        r_att = region(KC * ALL)
        xsq, attT = cut(r_att, 0, (KC, ALL)), cut(r_att, 0, (PAIRS, TOK))
        e_gate, e_up, e_sig, e_act = (cut(r_att, 512 * i, (8, CAP)) for i in range(4))
        r_rg = region(KC * TOK)
        rgT = cut(r_rg, 0, (KC, TOK))
        e_outT, e_out = cut(r_rg, 0, (KC, 2 * CAP)), cut(r_rg, 1024, (1024,))
        gate_sb = cut(region(4 * TOK), 0, (4, TOK))
        r_rq = region(RH * TOK + RH * ALL)
        rqT, rkT = cut(r_rq, 0, (RH, TOK)), cut(r_rq, RH * TOK, (RH, ALL))
        xeT = cut(r_rq, 0, (KC, CAP))
        sel, selw = cut(r_rq, 512, (2, 2 * CAP)), cut(r_rq, 768, (2, 2 * CAP))
        selwT = cut(r_rq, 1024, (TOK,))
        rt = 1280
        logits, chosen, wgt, posm = (cut(r_rq, rt + 64 * i, (2, EXPERTS)) for i in range(4))
        top8 = cut(r_rq, rt + 256, (2, 8))
        top8i = cut(r_rq, rt + 272, (2, 8)).bitcast(U32)
        top8f = cut(r_rq, rt + 288, (2, 8))
        neg_top, wsum, wrec = (cut(r_rq, rt + 304 + 2 * i, (2,)) for i in range(3))
        n_max, n_over, n_tmp = (cut(r_rq, rt + 310 + i, (1,)) for i in range(3))
        last_pair_i = cut(r_rq, rt + 314, (1,)).bitcast(I32)
        count = cut(r_rq, rt + 316, (EXPERTS,))
        wgtT = cut(r_rq, rt + 352, (TOK,), EXPERTS)
        r_rv = region(3 * D)
        kz = cut(r_rv, 0, (2, ALL))
        vz = cut(r_rv, 2 * ALL, (2, 2, P))
        vz_meta = cut(r_rv, 2 * ALL + 4 * P, (2, P), META)
        rv_tok, rv_meta = cut(r_rv, 0, (2, D)), cut(r_rv, 2 * D, (D,), META)
        hsq = cut(r_rv, 0, (KC, TOK))
        r_p = region(2 * 2 * SCW + 4 * BLK + 6 * BLK)
        prob = cut(r_p, 0, (2, 2, SCW))
        probT_meta = cut(r_p, 4 * SCW, (4, BLK), META)
        probT = cut(r_p, 4 * SCW + 4 * BLK, (6, BLK))
        rs, rs_meta = cut(r_p, 0, (RH, 3 * BLK)), cut(r_p, RH * 3 * BLK, (RH, TOK), META)
        tmp = cut(region(2 * 2 * TOK), 0, (2, 2 * TOK))
        sq = cut(region(2 * 2 * TOK), 0, (2, 2 * TOK))
        r_mix = region(ALL)
        root = region(ALL)
        par = region(N_PARAM)
        b_dn = cut(region(D), 0, (D,), EXPERTS)
        con = region(N_CONST)
        small = region(96)
        q_norm, q_rho, q_slope = (cut(small, 32 * i, (2, PAIRS, 2)) for i in range(3))
        v_tok = region(2)
        soft = region(40)
        s_max, s_neg, s_sink, s_esink, s_sum, s_den, s_rec = (cut(soft, 4 * i, (2, 2)) for i in range(7))

        def const(name, parts=P):
            at, n = CONST_COLS[name]
            return con[0:parts, at:at + n]

        def param(name):
            at, n = PARAM_COLS[name]
            return par[:, at:at + n]

        ones, ident = const("ones"), const("ident")
        decay = const("decay").rearrange("p (h q) -> p h q", h=RH)
        decay_meta = const("decay_meta", META).rearrange("p (h q) -> p h q", h=RH)
        sinks = param("sinks").rearrange("p (j x) -> p j x", x=2)
        w_rt = param("w_router").rearrange("p (k e) -> p k e", k=KC)
        b_gu = param("b_gate_up").rearrange("p (e c) -> p e c", e=EXPERTS)
        slopes = const("slopes").rearrange("p (b j x) -> p b j x", b=2, x=2)

        ps = ctx.enter_context(nc.psum_tensor("ps", [P, 8, 512], F32))
        PROJ, SCORE, PT_META, PT, PV = 0, 2, 4, 5, 7
        GATE, UP, GATHER, DOWN, Y = 0, 1, 2, 3, 4
        y_ps = ps[:, Y:Y + 4, :].rearrange("p b (c t) -> p (b c) t", t=TOK)

        landed = [sem(f"landed{i}") for i in range(SLOTS)]
        x_in = [sem("x_in0"), sem("x_in1")]
        early_in, params_in, late_in, bdown_in = sem("early_in"), sem("params_in"), sem("late_in"), sem("bdown_in")
        gained = sem("gained")
        squared = sem("squared")
        mix_stat = sem("mix_stat")
        mix_root = sem("mix_root")
        mix_r = sem("mix_r")
        zeros_set = sem("zeros_set")
        proj_done, proj_read = sem("proj_done"), sem("proj_read")
        k_sq, k_stat, k_root = sem("k_sq"), sem("k_stat"), sem("k_root")
        k_ready, v_turned, v_ready = sem("k_ready"), sem("v_turned"), sem("v_ready")
        q_sq, q_stat, q_root, q_ready = sem("q_sq"), sem("q_stat"), sem("q_root"), sem("q_ready")
        scored, score_read, biased = sem("scored"), sem("score_read"), sem("biased")
        exped, prob_ready = sem("exped"), sem("prob_ready")
        turned, turn_read, att_done, att_read = sem("turned"), sem("turn_read"), sem("att_done"), sem("att_read")
        sig_done = sem("sig_done")
        rv_turned, rv_read = sem("rv_turned"), sem("rv_read")
        rscored, rscore_read = sem("rscored"), sem("rscore_read")
        ret_done, ret_sq, ret_stat, ret_root, ret_ready = (sem("ret_done"), sem("ret_sq"), sem("ret_stat"),
                                                          sem("ret_root"), sem("ret_ready"))
        gate_sig = sem("gate_sig")
        h_sq, h_stat, h_root, u2_ready = sem("h_sq"), sem("h_stat"), sem("h_root"), sem("u2_ready")
        u2_turned, u2tok_ready = sem("u2_turned"), sem("u2tok_ready")
        logit_done, top_ready, route_exp = sem("logit_done"), sem("top_ready"), sem("route_exp")
        chosen_ready, counted, pairs_ready = sem("chosen_ready"), sem("counted"), sem("pairs_ready")
        wgt_ready, wgt_turned, wgtT_ready = sem("wgt_ready"), sem("wgt_turned"), sem("wgtT_ready")
        sel_ready, selw_ready = sem("sel_ready"), sem("selw_ready")
        units_used = sem("units_used")
        gathered, xe_ready = sem("gathered"), sem("xe_ready")
        gu_read, gate_ready, sig_ready, act_ready = (sem("gu_read"), sem("gate_ready"), sem("sig_ready"),
                                                     sem("act_ready"))
        out_read, out_turned, eout_ready = sem("out_read"), sem("out_turned"), sem("eout_ready")
        selw_turned, selwT_ready = sem("selw_turned"), sem("selwT_ready")
        scattered, final_ready, stored = sem("scattered"), sem("final_ready"), sem("stored")
        vec_step = sem("vec_step")

        block = ctx.enter_context(nc.Block())

        @block.sync
        def _(sp):
            for h in range(2):
                sp.dma_start(x_sb[:, 4 * h:4 * h + 4], xT[:, 4 * h:4 * h + 4]).then_inc(x_in[h], 16)
            for u in range(NU):
                if u >= SLOTS:
                    sp.wait_ge(proj_done, 2 * (u - SLOTS + 1))
                sp.dma_start(ring[:, u % SLOTS], mix_w[u]).then_inc(landed[u % SLOTS], 16)

            def expert_units(e, first_wait):
                for j in range(12):
                    first_wait(j)
                    slot = (NU + j) % SLOTS
                    if j < 8:
                        dst, src = ring[:, slot], w_gate_up[bass.ds(e, 1), j * P:(j + 1) * P, :].rearrange("o p n -> (o p) n")
                    else:
                        r = 2 * (j - 8) * P
                        dst = ring[:, slot].rearrange("p (c n) -> p c n", c=2)
                        src = w_down[bass.ds(e, 1), r:r + 2 * P, :].rearrange("o (c p) n -> (o p) c n", p=P)
                    sp.dma_start(dst, src).then_inc(landed[slot], 16)

            def pair_units(n, lap):
                for x in range(2):
                    def used(j, x=x):
                        if isinstance(n, int) and n == 0 and x == 0:
                            sp.wait_ge(proj_done, 2 * (NU + j - SLOTS + 1))
                        else:
                            sp.wait_ge(units_used, 24 * n + (12 * x + j - SLOTS + 1))
                    expert_units(2 * lap + x, used)

            pair_units(0, 0)
            with sp.Fori(1, 15) as n:
                pair_units(n, n)
            sp.wait_ge(pairs_ready, 1)
            final = sp.value_load(last_pair_i[0:1, :], min_val=15, max_val=63)
            with sp.Fori(15, final + 1) as n:
                lap = sp.compute_val(n & 15)
                pair_units(n, lap)
            for b in range(4):
                sp.wait_ge(final_ready, b + 1)
                sp.dma_start(out[:, 2 * b:2 * b + 2], x_sb[:, 2 * b:2 * b + 2, META:ALL]).then_inc(stored, 16)
            sp.wait_ge(stored, 64)

        @block.gpsimd
        def _(pool):
            empty = (kz[DH:P, 0, :], kz[0:DH, 1, :], vz[:, 0, :, DH:P], vz[:, 1, :, 0:DH],
                     vz_meta[:, 0, DH:P], vz_meta[:, 1, 0:DH])
            for n, v in enumerate(empty):
                if n >= 1:
                    pool.wait_ge(zeros_set, n)
                nc.gpsimd.memset(v, 0.0).then_inc(zeros_set, 1)

        @block.tensor
        def _(pe):
            mm, turn = nc.tensor.matmul, nc.tensor.transpose

            def project(c):
                kind, i = CHUNKS[c]
                unit, half = divmod(c, 2)
                if half == 0:
                    pe.wait_ge(landed[unit % SLOTS], 16 * (unit // SLOTS + 1))
                if c >= 2:
                    pe.wait_ge(proj_read, c - 1)
                if kind == "wa" and i == 0:
                    pe.wait_ge(att_read, PAIRS)
                if kind == "wr" and i == 0:
                    pe.wait_ge(ret_ready, RH)
                if kind == "out" and i == 0:
                    pe.wait_ge(proj_read, c)
                w = ring[:, unit % SLOTS].rearrange("p (k n) -> p k n", k=KC)
                for k in range(KC):
                    if kind == "wa":
                        rhs = attT[:, k]
                    elif kind == "wr":
                        rhs = rgT[:, k]
                    elif kind == "out":
                        rhs = merged[:, k]
                    elif kind in ("k", "v", "rk", "rv"):
                        rhs = u_sb[:, k]
                    else:
                        rhs = u_sb[:, k, META:ALL]
                    last = mm(ps[:, PROJ + half, 0:rhs.shape[-1]], w[:, k, half * P:(half + 1) * P], rhs,
                              start=(k == 0), stop=(k == KC - 1))
                last.then_inc(proj_done, 1)

            def mix_stats():
                for k in range(KC):
                    if k % 4 == 0:
                        pe.wait_ge(squared, k // 4 + 1)
                    last = mm(ps[:, SCORE, 0:ALL], ones, xsq[:, k], start=(k == 0), stop=(k == KC - 1))
                last.then_inc(mix_stat, 1)
                for b in range(2):
                    for k in range(KC):
                        last = mm(ps[:, PV, 32 + b:33 + b], xsq[:, k, META + b * BLK:META + (b + 1) * BLK],
                                  ones[:, 0:1], start=(k == 0), stop=(k == KC - 1))
                last.then_inc(mix_stat, 1)

            def q_stats(j):
                pe.wait_ge(q_sq, j + 1)
                for b in range(2):
                    at = b * HEADS + 2 * j
                    last = mm(ps[:, PV, at:at + 2], sq[:, j % 2, b * BLK:(b + 1) * BLK], const("halves"),
                              start=True, stop=True)
                last.then_inc(q_stat, 1)

            def scores(j):
                if j == 0:
                    pe.wait_ge(q_ready, 1)
                    pe.wait_ge(k_ready, 2)
                    pe.wait_ge(zeros_set, 6)
                else:
                    pe.wait_ge(score_read, j)
                for x in range(2):
                    mm(ps[:, SCORE + x, 0:B1K], qT[:, j, 0:BLK], kz[:, x, 0:B1K], start=True, stop=True)
                    last = mm(ps[:, SCORE + x, B1K:SCW], qT[:, j, BLK:TOK], kz[:, x, :], start=True, stop=True)
                last.then_inc(scored, 1)

            def turn_probs(j):
                pe.wait_ge(prob_ready, j + 1)
                if j >= 1:
                    pe.wait_ge(turn_read, j)
                for x in range(2):
                    p_x = prob[:, j % 2, x]
                    for b, at in ((0, 0), (1, B1K)):
                        turn(ps[0:META, PT_META, (2 * b + x) * BLK:(2 * b + x + 1) * BLK], p_x[:, at:at + META], ident)
                    for c, at in enumerate((META, B1K + META, B1K + META + BLK)):
                        last = turn(ps[:, PT + x, c * BLK:(c + 1) * BLK], p_x[:, at:at + BLK], ident)
                last.then_inc(turned, 1)

            def attend(j):
                if j == 0:
                    pe.wait_ge(v_ready, 4)
                    pe.wait_ge(q_root, 2)
                else:
                    pe.wait_ge(att_read, j)
                pe.wait_ge(turn_read, j + 1)
                for b in range(2):
                    o = ps[:, PV, b * BLK:(b + 1) * BLK]
                    for x in range(2):
                        mm(o, vz_meta[:, x], probT_meta[:, 2 * b + x], start=(x == 0), stop=False)
                        for c in range(b + 1):
                            last = mm(o, vz[:, x, c], probT[:, 3 * x + b + c], start=False, stop=(x == 1 and c == b))
                last.then_inc(att_done, 1)

            def turn_value(i):
                bank = PT_META + i % 2
                pe.wait_ge(proj_read, AT[("rv", i)] + 1)
                if i >= 2:
                    pe.wait_ge(rv_read, i - 1)
                t = tmp[:, i % 2]
                turn(ps[0:META, bank, 0:P], t[:, 0:META], ident)
                turn(ps[:, bank, P:2 * P], t[:, META:META + BLK], ident)
                turn(ps[:, bank, 2 * P:3 * P], t[:, META + BLK:ALL], ident).then_inc(rv_turned, 1)

            def ret_scores(h):
                if h == 0:
                    pe.wait_ge(score_read, PAIRS)
                else:
                    pe.wait_ge(rscore_read, h)
                q = rqT[:, h]
                mm(ps[:, SCORE, 0:TOK], rkT[:, h, META:META + BLK], q, start=True, stop=True)
                mm(ps[:, SCORE, TOK:TOK + BLK], rkT[:, h, META + BLK:ALL], q[:, BLK:TOK], start=True, stop=True)
                mm(ps[0:META, SCORE + 1, 0:TOK], rkT[:, h, 0:META], q, start=True, stop=True).then_inc(rscored, 1)

            def ret_bank(h):
                return (SCORE, SCORE + 1, PT + 1, PV)[h]

            def retain(h):
                pe.wait_ge(rscore_read, RH)
                pe.wait_ge(rv_read, 2 * RH)
                bank = ret_bank(h)
                for v in range(2):
                    f = slice((2 * h + v) * P, (2 * h + v + 1) * P)
                    o = ps[:, bank, v * TOK:(v + 1) * TOK]
                    mm(o, rv_meta[:, f], rs_meta[:, h], start=True, stop=False, skip_group_check=True)
                    mm(o, rv_tok[:, 0, f], rs[:, h, 0:TOK], start=False, stop=False, skip_group_check=True)
                    last = mm(o[:, BLK:TOK], rv_tok[:, 1, f], rs[:, h, TOK:TOK + BLK], start=False, stop=True,
                              skip_group_check=True)
                last.then_inc(ret_done, 1)

            def ret_stats(h):
                pe.wait_ge(ret_sq, h + 1)
                bank = PT_META + h % 2
                if h >= 2:
                    pe.wait_ge(ret_root, h - 1)
                for v in range(2):
                    last = mm(ps[:, bank, 0:TOK], ones, sq[:, h % 2, v * TOK:(v + 1) * TOK], start=(v == 0), stop=(v == 1))
                last.then_inc(ret_stat, 1)

            pe.wait_ge(early_in, 16)
            mix_stats()
            pe.wait_ge(gained, 2)
            project(0)
            project(1)
            project(2)
            pe.wait_ge(k_sq, 1)
            mm(ps[:, PT + 1, 0:ALL], const("heads2"), sq[:, 0, 0:ALL], start=True, stop=True).then_inc(k_stat, 1)
            pe.wait_ge(proj_read, AT[("v", 0)] + 1)
            turn(ps[0:META, PT_META, 0:P], tmp[:, 1, 0:META], ident)
            turn(ps[:, PT, 0:P], tmp[:, 1, META:META + BLK], ident)
            turn(ps[:, PT, P:2 * P], tmp[:, 1, META + BLK:ALL], ident).then_inc(v_turned, 1)
            for j in range(PAIRS):
                project(AT[("q", j)] + 1)
                q_stats(j)
            for i in range(PAIRS + 1):
                c = AT[("rq", 0)] + 2 * i
                if i > 0:
                    project(c)
                    turn_probs(i - 1)
                if i < PAIRS:
                    scores(i)
                project(c + 1)
                if i > 0:
                    attend(i - 1)
            project(AT[("ga", 2)])
            project(AT[("ga", 3)])
            for h in range(RH):
                project(AT[("rv", 2 * h)])
                if h > 0:
                    turn_value(2 * h - 1)
                ret_scores(h)
                project(AT[("rv", 2 * h + 1)])
                turn_value(2 * h)
            project(AT[("wa", 0)])
            turn_value(2 * RH - 1)
            project(AT[("wa", 1)])
            retain(0)
            retain(1)
            project(AT[("wa", 2)])
            ret_stats(0)
            retain(2)
            project(AT[("wa", 3)])
            ret_stats(1)
            retain(3)
            project(AT[("ga", 4)])
            ret_stats(2)
            project(AT[("ga", 5)])
            ret_stats(3)
            for c in range(AT[("ga", 5)] + 1, len(CHUNKS)):
                project(c)

            for k in range(KC):
                pe.wait_ge(h_sq, k + 1)
                last = mm(ps[:, SCORE, 0:TOK], ones, hsq[:, k], start=(k == 0), stop=(k == KC - 1))
            last.then_inc(h_stat, 1)
            pe.wait_ge(u2_ready, KC)
            for t in range(2):
                for k in range(KC):
                    last = mm(ps[:, DOWN, t * EXPERTS:(t + 1) * EXPERTS], u2T[:, k, t * P:(t + 1) * P], w_rt[:, k],
                              start=(k == 0), stop=(k == KC - 1))
            last.then_inc(logit_done, 1)
            for t in range(2):
                for k in range(KC):
                    last = turn(ps[:, Y + 2 * t + k // 4, (k % 4) * P:(k % 4 + 1) * P], u2T[:, k, t * P:(t + 1) * P], ident)
                last.then_inc(u2_turned, 1)
            pe.wait_ge(chosen_ready, 1)
            mm(ps[:, GATE, 0:EXPERTS], const("tri"), chosen[:, 0], start=True, stop=True)
            mm(ps[:, GATE, EXPERTS:2 * EXPERTS], ones, chosen[:, 0], start=True, stop=False)
            mm(ps[:, GATE, EXPERTS:2 * EXPERTS], const("tri"), chosen[:, 1], start=False, stop=True)
            mm(ps[:, GATE, 2 * EXPERTS:3 * EXPERTS], ones, chosen[:, 0], start=True, stop=False)
            mm(ps[:, GATE, 2 * EXPERTS:3 * EXPERTS], ones, chosen[:, 1], start=False, stop=True).then_inc(counted, 1)
            pe.wait_ge(wgt_ready, 1)
            for t in range(2):
                last = turn(ps[0:EXPERTS, UP, t * P:(t + 1) * P], wgt[:, t], ident)
            last.then_inc(wgt_turned, 1)
            pe.wait_ge(wgtT_ready, 1)
            pe.wait_ge(bdown_in, 16)
            pe.wait_ge(u2tok_ready, 2)
            for c in range(KC):
                mm(y_ps[:, c], b_dn[:, c * P:(c + 1) * P], wgtT, start=(c % 2 == 0), stop=False, skip_group_check=True)

            def gather(x, E):
                for k in range(KC):
                    for t in range(2):
                        last = mm(ps[:, GATHER, k * CAP:(k + 1) * CAP], u2tok[:, t, k * P:(k + 1) * P],
                                  sel[:, t, x * CAP:(x + 1) * CAP], start=(t == 0), stop=(t == 1))
                last.then_inc(gathered, 1)

            def gate_up(E, n_expr):
                pe.wait_ge(xe_ready, n_expr + 1)
                if not (isinstance(n_expr, int) and n_expr == 0):
                    pe.wait_ge(gu_read, n_expr)
                for j in range(8):
                    slot = (NU + j) % SLOTS
                    pe.wait_ge(landed[slot], 16 * n_expr + 16 * ((NU + j) // SLOTS + 1))
                    for m in range(16):
                        last = mm(ps[:, GATE + m // 8, (m % 8) * CAP:(m % 8 + 1) * CAP],
                                  ring[:, slot, m * P:(m + 1) * P], xeT[:, j],
                                  start=(j == 0 and m % 8 == 0), stop=(j == 7), skip_group_check=True)
                    last.then_inc(units_used, 1)

            def down(n_expr):
                pe.wait_ge(act_ready, n_expr + 1)
                for j in range(8, 12):
                    slot = (NU + j) % SLOTS
                    pe.wait_ge(landed[slot], 16 * n_expr + 16 * ((NU + j) // SLOTS + 1))
                    for f in range(2):
                        k = 2 * (j - 8) + f
                        for m in range(8):
                            last = mm(ps[:, DOWN, m * CAP:(m + 1) * CAP],
                                      ring[:, slot, f * 1024 + m * P:f * 1024 + (m + 1) * P], e_act[:, k],
                                      start=(k == 0 and m == 0), stop=(k == 7), skip_group_check=True)
                    last.then_inc(units_used, 1)

            def add_back(n):
                pe.wait_ge(out_read, 2 * n)
                for k in range(KC):
                    last = turn(ps[:, GATHER + k // 4, (k % 4) * P:(k % 4 + 1) * P], e_outT[:, k], ident)
                last.then_inc(out_turned, 1)
                pe.wait_ge(selwT_ready, n)
                pe.wait_ge(eout_ready, n)
                for c in range(KC):
                    last = mm(y_ps[:, c], e_out[:, c * P:(c + 1) * P], selwT, start=False, stop=False,
                              skip_group_check=True)
                last.then_inc(scattered, 1)

            def pair(n, first, last_pair):
                gate_up(0, 2 * n)
                if not first:
                    add_back(n)
                gather(1, 0)
                down(2 * n)
                gate_up(1, 2 * n + 1)
                pe.wait_ge(selw_ready, n + 1)
                pe.wait_ge(out_read, 2 * n + 1)
                for t in range(2):
                    o = turn(ps[:, DOWN, t * P:(t + 1) * P], selw[:, t], ident)
                o.then_inc(selw_turned, 1)
                if not last_pair:
                    pe.wait_ge(sel_ready, n + 2)
                    pe.wait_ge(xe_ready, 2 * n + 2)
                    gather(0, 0)
                pe.wait_ge(selwT_ready, n + 1)
                down(2 * n + 1)

            pe.wait_ge(pairs_ready, 1)
            final = pe.value_load(last_pair_i[0:1, :], min_val=15, max_val=63)
            pe.wait_ge(sel_ready, 1)
            gather(0, 0)
            pair(0, True, False)
            with pe.Fori(1, final) as n:
                pair(n, False, False)
            pair(final, False, True)
            add_back(final + 1)

        @block.scalar
        def _(act):
            A = nc.scalar.activation
            act.dma_start(con[:, 0:N_CONST_EARLY], consts[:, 0:N_CONST_EARLY]).then_inc(early_in, 16)
            act.dma_start(par, params).then_inc(params_in, 16)
            act.dma_start(con[:, N_CONST_EARLY:N_CONST], consts[:, N_CONST_EARLY:N_CONST]).then_inc(late_in, 16)
            act.dma_start(b_dn, b_down).then_inc(bdown_in, 16)
            for h in range(2):
                act.wait_ge(x_in[h], 16)
                A(xsq[:, 4 * h:4 * h + 4], x_sb[:, 4 * h:4 * h + 4], ACT.Square).then_inc(squared, 1)
            act.wait_ge(early_in, 16)
            act.wait_ge(mix_stat, 2)
            A(root, ps[:, SCORE, 0:ALL], ACT.Sqrt, bias=const("eps"), scale=1.0 / D).then_inc(mix_root, 1)
            A(v_tok, ps[:, PV, 32:34], ACT.Copy, scale=1.0 / D).then_inc(mix_root, 1)
            act.wait_ge(params_in, 16)
            act.wait_ge(proj_read, 1)
            A(sq[:, 0, 0:ALL], tmp[:, 0, 0:ALL], ACT.Square).then_inc(k_sq, 1)

            def query(j):
                c = AT[("q", j)]
                act.wait_ge(proj_done, c + 1)
                if j >= 2:
                    act.wait_ge(q_stat, j - 1)
                if j == 0:
                    act.wait_ge(k_stat, 1)
                A(sq[:, j % 2, 0:TOK], ps[:, PROJ + c % 2, 0:TOK], ACT.Square).then_inc(q_sq, 1)
                act.wait_ge(proj_read, c)
                A(qT[:, j], ps[:, PROJ + c % 2, 0:TOK], ACT.Copy, scale=param("q_gain")).then_inc(proj_read, 1)

            query(0)
            act.wait_ge(mix_r, 1)
            A(root, ps[:, PT + 1, 0:ALL], ACT.Sqrt, bias=const("eps"), scale=1.0 / DH).then_inc(k_root, 1)
            act.wait_ge(v_turned, 1)
            act.wait_ge(zeros_set, 6)
            for x in range(2):
                f = slice(x * DH, (x + 1) * DH)
                A(vz_meta[:, x, f], ps[0:META, PT_META, f], ACT.Copy).then_inc(v_ready, 1)
                A(vz[:, x, :, f], ps[:, PT, 0:2 * P].rearrange("p (c f) -> p c f", c=2)[:, :, f],
                  ACT.Copy).then_inc(v_ready, 1)
            for j in range(1, PAIRS):
                query(j)
            act.wait_ge(q_stat, PAIRS)
            act.wait_ge(mix_r, 2)
            for b in range(2):
                A(q_norm[:, b], ps[:, PV, b * HEADS:(b + 1) * HEADS].rearrange("p (j x) -> p j x", x=2), ACT.Sqrt,
                  bias=v_tok[:, b:b + 1]).then_inc(q_root, 1)

            for i in range(PAIRS + 1):
                if i > 0:
                    j = i - 1
                    act.wait_ge(turned, j + 1)
                    if j >= 1:
                        act.wait_ge(att_done, j)
                    A(probT_meta, ps[0:META, PT_META].rearrange("p (a b) -> p a b", b=BLK), ACT.Copy)
                    A(probT.rearrange("p (x c) q -> p x (c q)", x=2), ps[:, PT:PT + 2, 0:3 * BLK],
                      ACT.Copy).then_inc(turn_read, 1)
                if i < PAIRS:
                    act.wait_ge(biased, i + 1)
                    for x in range(2):
                        for b, (lo, hi) in enumerate(((0, B1K), (B1K, SCW))):
                            v = prob[:, i % 2, x, lo:hi]
                            A(v, v, ACT.Exp, bias=s_neg[:, b, x:x + 1], scale=q_rho[:, b, i, x:x + 1],
                              accum_out=s_sum[:, b, x:x + 1])
                    A(s_esink, s_sink, ACT.Exp).then_inc(exped, 1)
                if i > 0:
                    act.wait_ge(att_done, i)
                    A(attT[:, i - 1], ps[:, PV, 0:TOK], ACT.Copy).then_inc(att_read, 1)

            act.wait_ge(proj_read, AT[("ga", 3)] + 1)
            for h in range(RH):
                A(sig_rg[:, 2 * h:2 * h + 2], rgT[:, 2 * h:2 * h + 2], ACT.Sigmoid).then_inc(sig_done, 1)
            A(gate_sb, gate_sb, ACT.Sigmoid).then_inc(gate_sig, 4)

            def value_read(i):
                act.wait_ge(rv_turned, i + 1)
                bank = PT_META + i % 2
                f = slice(i * P, (i + 1) * P)
                A(rv_meta[:, f], ps[0:META, bank, 0:P], ACT.Copy)
                A(rv_tok[:, :, f], ps[:, bank, P:3 * P].rearrange("p (c f) -> p c f", c=2), ACT.Copy).then_inc(rv_read, 1)

            for i in range(2 * RH):
                value_read(i)

            def ret_bank(h):
                return (SCORE, SCORE + 1, PT + 1, PV)[h]

            def ret_square(h):
                act.wait_ge(ret_done, h + 1)
                if h >= 2:
                    act.wait_ge(ret_stat, h - 1)
                A(sq[:, h % 2], ps[:, ret_bank(h)], ACT.Square).then_inc(ret_sq, 1)

            def ret_sqrt(h):
                act.wait_ge(ret_stat, h + 1)
                if h >= 1:
                    act.wait_ge(ret_ready, h)
                A(root[:, 0:TOK], ps[:, PT_META + h % 2, 0:TOK], ACT.Sqrt, bias=const("eps"),
                  scale=1.0 / RDV).then_inc(ret_root, 1)

            ret_square(0)
            ret_square(1)
            ret_sqrt(0)
            ret_square(2)
            ret_sqrt(1)
            ret_square(3)
            ret_sqrt(2)
            ret_sqrt(3)
            for kind in ("ga", "gr"):
                for i in range(4 if kind == "ga" else 0, KC):
                    act.wait_ge(proj_read, AT[(kind, i)] + 1)
                    A(gate_sb[:, i % 4], gate_sb[:, i % 4], ACT.Sigmoid).then_inc(gate_sig, 1)
            for k in range(KC):
                act.wait_ge(proj_read, AT[("out", k)] + 1)
                A(hsq[:, k], x_sb[:, k, META:ALL], ACT.Square).then_inc(h_sq, 1)
            act.wait_ge(h_stat, 1)
            A(root[:, 0:TOK], ps[:, SCORE, 0:TOK], ACT.Sqrt, bias=const("eps"), scale=1.0 / D).then_inc(h_root, 1)
            for t in range(2):
                act.wait_ge(u2_turned, t + 1)
                A(u2tok[:, t].rearrange("p (b f) -> p b f", b=2), ps[:, Y + 2 * t:Y + 2 * t + 2], ACT.Copy).then_inc(u2tok_ready, 1)
            act.wait_ge(top_ready, 1)
            for t in range(2):
                A(wgt[:, t], logits[:, t], ACT.Exp, bias=neg_top[:, t:t + 1]).then_inc(route_exp, 1)
            act.wait_ge(wgt_turned, 1)
            A(wgtT, ps[0:EXPERTS, UP, 0:TOK], ACT.Copy).then_inc(wgtT_ready, 1)

            def sigmoid(E):
                act.wait_ge(gate_ready, E + 1)
                A(e_sig, e_gate, ACT.Sigmoid, scale=ALPHA).then_inc(sig_ready, 1)

            def outputs(x, E):
                act.wait_ge(units_used, 12 * E + 12)
                A(e_outT[:, :, x * CAP:(x + 1) * CAP], ps[:, DOWN].rearrange("p (k s) -> p k s", k=KC),
                  ACT.Copy).then_inc(out_read, 1)

            def outputs_by_slot(n):
                act.wait_ge(out_turned, n)
                A(e_out.rearrange("p (b f) -> p b f", b=2), ps[:, GATHER:GATHER + 2], ACT.Copy).then_inc(eout_ready, 1)

            def pair(n, first):
                if not first:
                    outputs_by_slot(n)
                sigmoid(2 * n)
                outputs(0, 2 * n)
                act.wait_ge(selw_turned, n + 1)
                A(selwT, ps[:, DOWN, 0:TOK], ACT.Copy).then_inc(selwT_ready, 1)
                sigmoid(2 * n + 1)
                outputs(1, 2 * n + 1)

            act.wait_ge(pairs_ready, 1)
            final = act.value_load(last_pair_i[0:1, :], min_val=15, max_val=63)
            pair(0, True)
            with act.Fori(1, final + 1) as n:
                pair(n, False)
            outputs_by_slot(final + 1)

        @block.vector
        def _(dve):
            V = nc.vector
            steps = [0]

            def link(ins):
                steps[0] += 1
                ins.then_inc(vec_step, 1)
                dve.wait_ge(vec_step, steps[0])

            dve.wait_ge(params_in, 16)
            for h in range(2):
                dve.wait_ge(x_in[h], 16)
                for k in range(4 * h, 4 * h + 4):
                    last = V.tensor_scalar(u_sb[:, k], x_sb[:, k], param("mix_gain")[:, k:k + 1], None, ALU.mult)
                last.then_inc(gained, 1)
            dve.wait_ge(mix_root, 2)
            V.reciprocal(r_mix, root).then_inc(mix_r, 1)
            V.tensor_scalar(v_tok, v_tok, EPS, DH * EPS, ALU.add, ALU.mult).then_inc(mix_r, 1)
            dve.wait_ge(mix_r, 2)

            def evict(c, dst):
                n = dst.shape[-1]
                dve.wait_ge(proj_done, c + 1)
                V.tensor_tensor(dst, ps[:, PROJ + c % 2, 0:n], r_mix[:, ALL - n:ALL], ALU.mult).then_inc(proj_read, 1)

            evict(0, tmp[:, 0, 0:ALL])
            evict(1, tmp[:, 1, 0:ALL])
            dve.wait_ge(k_root, 1)
            dve.wait_ge(proj_read, 2)
            link(V.reciprocal(root, root))
            dve.wait_ge(zeros_set, 6)
            for x in range(2):
                f = slice(x * DH, (x + 1) * DH)
                V.scalar_tensor_tensor(kz[f, x], tmp[f, 0, 0:ALL], param("k_gain")[f], root[f], ALU.mult,
                                       ALU.mult).then_inc(k_ready, 1)
            dve.wait_ge(q_root, 2)
            V.reciprocal(q_rho, q_norm).then_inc(q_ready, 1)
            dve.wait_ge(late_in, 16)
            link(V.tensor_tensor(q_slope, q_norm, slopes, ALU.mult))

            def place_of(c):
                kind, i = CHUNKS[c]
                return {"rq": rqT, "rk": rkT, "rg": rgT, "ga": gate_sb}[kind][:, i]

            def bias_scores(i):
                dve.wait_ge(scored, i + 1)
                for x in range(2):
                    for b, (lo, hi) in enumerate(((0, B1K), (B1K, SCW))):
                        last = V.scalar_tensor_tensor(prob[:, i % 2, x, lo:hi], const("alibi")[:, lo:hi],
                                                      q_slope[:, b, i, x:x + 1], ps[:, SCORE + x, lo:hi],
                                                      ALU.mult, ALU.add)
                last.then_inc(score_read, 1)
                dve.wait_ge(score_read, i + 1)
                V.tensor_reduce(s_max[:, 0], prob[:, i % 2, :, 0:B1K], AX.X, ALU.max)
                link(V.tensor_reduce(s_max[:, 1], prob[:, i % 2, :, B1K:SCW], AX.X, ALU.max))
                link(V.tensor_tensor(s_max, s_max, q_rho[:, :, i], ALU.mult))
                sink = sinks[:, i:i + 1].to_broadcast([P, 2, 2])
                link(V.tensor_tensor(s_max, s_max, sink, ALU.max))
                if i >= 1:
                    dve.wait_ge(exped, i)
                V.tensor_scalar(s_neg, s_max, -1.0, None, ALU.mult)
                V.tensor_tensor(s_sink, sink, s_max, ALU.subtract).then_inc(biased, 1)

            def normalise(i):
                dve.wait_ge(exped, i + 1)
                link(V.tensor_tensor(s_den, s_sum, s_esink, ALU.add))
                link(V.reciprocal(s_rec, s_den))
                for x in range(2):
                    for b, (lo, hi) in enumerate(((0, B1K), (B1K, SCW))):
                        v = prob[:, i % 2, x, lo:hi]
                        last = V.tensor_scalar(v, v, s_rec[:, b, x:x + 1], None, ALU.mult)
                last.then_inc(prob_ready, 1)

            evict_first = AT[("rq", 0)]
            dve.wait_ge(proj_read, evict_first)
            for i in range(PAIRS + 1):
                c = AT[("rq", 0)] + 2 * i
                evict(c, place_of(c))
                if i < PAIRS:
                    bias_scores(i)
                evict(c + 1, place_of(c + 1))
                if i < PAIRS:
                    normalise(i)
            evict(AT[("ga", 2)], gate_sb[:, 2])
            evict(AT[("ga", 3)], gate_sb[:, 3])
            for h in range(RH):
                for v in range(2):
                    i = 2 * h + v
                    if i >= 2:
                        dve.wait_ge(rv_turned, i - 1)
                    if i == 0:
                        dve.wait_ge(att_done, PAIRS)
                    evict(AT[("rv", i)], tmp[:, i % 2, 0:ALL])
                    if v == 0:
                        dve.wait_ge(rscored, h + 1)
                        V.tensor_tensor(rs[:, h, 0:TOK], ps[:, SCORE, 0:TOK], decay[:, h], ALU.mult)
                        V.tensor_tensor(rs[:, h, TOK:TOK + BLK], ps[:, SCORE, TOK:TOK + BLK], decay[:, h, 0:BLK], ALU.mult)
                        V.tensor_tensor(rs_meta[:, h], ps[0:META, SCORE + 1, 0:TOK], decay_meta[:, h],
                                        ALU.mult).then_inc(rscore_read, 1)
                dve.wait_ge(sig_done, h + 1)
                link(V.tensor_tensor(rgT[:, 2 * h:2 * h + 2], rgT[:, 2 * h:2 * h + 2], sig_rg[:, 2 * h:2 * h + 2], ALU.mult))

            def ret_out(h):
                bank = (SCORE, SCORE + 1, PT + 1, PV)[h]
                dve.wait_ge(ret_root, h + 1)
                rr = tmp[:, 0, 0:TOK]
                link(V.reciprocal(rr, root[:, 0:TOK]))
                g = rgT[:, 2 * h:2 * h + 2]
                link(V.tensor_tensor(g, g, rr.rearrange("p (o t) -> p o t", o=1).to_broadcast([P, 2, TOK]), ALU.mult))
                V.tensor_tensor(g, g, ps[:, bank].rearrange("p (v t) -> p v t", v=2), ALU.mult).then_inc(ret_ready, 1)

            def merge(c):
                kind, i = CHUNKS[c]
                b = ps[:, PROJ + c % 2, 0:TOK]
                if kind in ("ga", "gr"):
                    if i >= 4 or kind == "gr":
                        evict(c, gate_sb[:, i % 4])
                elif kind == "wa":
                    dve.wait_ge(gate_sig, i + 1)
                    dve.wait_ge(proj_done, c + 1)
                    V.tensor_tensor(merged[:, i], b, gate_sb[:, i % 4], ALU.mult).then_inc(proj_read, 1)
                elif kind == "wr":
                    dve.wait_ge(gate_sig, KC + i + 1)
                    dve.wait_ge(proj_done, c + 1)
                    gated = tmp[:, (i + 1) % 2, 0:TOK]
                    link(V.tensor_tensor(gated, b, gate_sb[:, i % 4], ALU.mult))
                    V.tensor_tensor(merged[:, i], merged[:, i], gated, ALU.add).then_inc(proj_read, 1)
                elif kind == "out":
                    dve.wait_ge(proj_done, c + 1)
                    h = x_sb[:, i, META:ALL]
                    V.tensor_tensor(h, h, b, ALU.add).then_inc(proj_read, 1)

            for c in range(AT[("wa", 0)], len(CHUNKS)):
                merge(c)
                if c == AT[("wa", 3)]:
                    ret_out(0)
                if c == AT[("ga", 4)]:
                    ret_out(1)
                if c == AT[("ga", 5)]:
                    ret_out(2)
                if c == AT[("ga", 5)] + 1:
                    ret_out(3)

            dve.wait_ge(h_root, 1)
            dve.wait_ge(proj_read, len(CHUNKS))
            r2 = tmp[:, 0, 0:TOK]
            link(V.reciprocal(r2, root[:, 0:TOK]))
            for k in range(KC):
                V.scalar_tensor_tensor(u2T[:, k], x_sb[:, k, META:ALL], param("ffn_gain")[:, k:k + 1], r2, ALU.mult,
                                       ALU.mult).then_inc(u2_ready, 1)
            dve.wait_ge(logit_done, 1)
            br = param("b_router").rearrange("p (o e) -> p o e", o=1).to_broadcast([P, 2, EXPERTS])
            link(V.tensor_tensor(logits, ps[:, DOWN, 0:2 * EXPERTS].rearrange("p (t e) -> p t e", t=2), br, ALU.add))
            for t in range(2):
                link(V.max(top8[:, t], logits[:, t]))
            V.tensor_scalar(neg_top, top8[:, :, 0], -1.0, None, ALU.mult).then_inc(top_ready, 1)
            for t in range(2):
                link(V.max_index(top8i[:, t], top8[:, t], logits[:, t]))
            link(V.tensor_copy(top8f, top8i))
            i32 = const("iota")[:, 0:EXPERTS]
            for t in range(2):
                link(V.tensor_scalar(chosen[:, t], i32, top8f[:, t, 0:1], None, ALU.is_equal))
                for r in range(1, TOPK):
                    ins = V.scalar_tensor_tensor(chosen[:, t], i32, top8f[:, t, r:r + 1], chosen[:, t], ALU.is_equal, ALU.add)
                    if t == 1 and r == TOPK - 1:
                        ins.then_inc(chosen_ready, 1)
                        dve.wait_ge(chosen_ready, 1)
                    else:
                        link(ins)
            dve.wait_ge(route_exp, 2)
            link(V.tensor_tensor(wgt, wgt, chosen, ALU.mult))
            link(V.tensor_reduce(wsum, wgt, AX.X, ALU.add))
            link(V.reciprocal(wrec, wsum))
            V.tensor_scalar(wgt[:, 0], wgt[:, 0], wrec[:, 0:1], None, ALU.mult)
            V.tensor_scalar(wgt[:, 1], wgt[:, 1], wrec[:, 1:2], None, ALU.mult).then_inc(wgt_ready, 1)
            dve.wait_ge(counted, 1)
            pos = ps[:, GATE, 0:2 * EXPERTS].rearrange("p (t e) -> p t e", t=2)
            link(V.scalar_tensor_tensor(posm, pos, 1.0, chosen, ALU.add, ALU.mult))
            link(V.tensor_scalar(posm, posm, -1.0, None, ALU.add))
            link(V.tensor_copy(count, ps[:, GATE, 2 * EXPERTS:3 * EXPERTS]))
            link(V.tensor_reduce(n_max, count, AX.X, ALU.max))
            link(V.tensor_scalar(n_over, n_max, float(CAP), 16.0, ALU.is_gt, ALU.mult))
            for r in (2, 3):
                link(V.tensor_scalar(n_tmp, n_max, float(r * CAP), 16.0, ALU.is_gt, ALU.mult))
                link(V.tensor_tensor(n_over, n_over, n_tmp, ALU.add))
            V.tensor_scalar(last_pair_i, n_over, 15.0, None, ALU.add).then_inc(pairs_ready, 1)

            def select(lap, rnd):
                place = posm[:, :, bass.ds(2 * lap, 2)]
                col = const("iota")[:, bass.ds(CAP * rnd, CAP)]
                V.tensor_tensor(sel.rearrange("p t (x s) -> p t x s", x=2),
                                col.rearrange("p (a b s) -> p a b s", a=1, b=1).to_broadcast([P, 2, 2, CAP]),
                                place.rearrange("p t (x o) -> p t x o", o=1).to_broadcast([P, 2, 2, CAP]),
                                ALU.is_equal).then_inc(sel_ready, 1)

            def weigh(n, lap):
                w = wgt[:, :, bass.ds(2 * lap, 2)]
                dve.wait_ge(sel_ready, n + 1)
                V.tensor_tensor(selw.rearrange("p t (x s) -> p t x s", x=2), sel.rearrange("p t (x s) -> p t x s", x=2),
                                w.rearrange("p t (x o) -> p t x o", o=1).to_broadcast([P, 2, 2, CAP]),
                                ALU.mult).then_inc(selw_ready, 1)

            def columns_read(E):
                dve.wait_ge(gathered, E + 1)
                V.tensor_copy(xeT, ps[:, GATHER].rearrange("p (k s) -> p k s", k=KC)).then_inc(xe_ready, 1)

            def hidden(E, e, step):
                def link(ins, k):
                    ins.then_inc(vec_step, 1)
                    dve.wait_ge(vec_step, step + k)

                def bias(half):
                    return b_gu[:, bass.ds(e, 1), 8 * half:8 * half + 8].rearrange("p o (k s) -> p (o k) s", s=1).to_broadcast([P, 8, CAP])

                dve.wait_ge(units_used, 12 * E + 8)
                link(V.tensor_tensor(e_gate, ps[:, GATE].rearrange("p (k s) -> p k s", k=8), bias(0), ALU.add), 1)
                V.tensor_scalar(e_gate, e_gate, LIMIT, None, ALU.min).then_inc(gate_ready, 1)
                V.tensor_tensor(e_up, ps[:, UP].rearrange("p (k s) -> p k s", k=8), bias(1), ALU.add).then_inc(gu_read, 1)
                dve.wait_ge(gu_read, E + 1)
                link(V.tensor_scalar(e_up, e_up, LIMIT, -LIMIT, ALU.min, ALU.max), 2)
                link(V.scalar_tensor_tensor(e_up, e_up, 1.0, e_gate, ALU.add, ALU.mult), 3)
                dve.wait_ge(sig_ready, E + 1)
                V.tensor_tensor(e_act, e_up, e_sig, ALU.mult).then_inc(act_ready, 1)

            step0 = steps[0]

            def pair(n, lap, next_lap, next_rnd, last_pair):
                step = 6 * n + step0
                hidden(2 * n, 2 * lap, step)
                columns_read(2 * n + 1)
                weigh(n, lap)
                if not last_pair:
                    dve.wait_ge(selw_ready, n + 1)
                    select(next_lap, next_rnd)
                hidden(2 * n + 1, 2 * lap + 1, step + 3)
                if not last_pair:
                    columns_read(2 * n + 2)

            dve.wait_ge(pairs_ready, 1)
            final = dve.value_load(last_pair_i[0:1, :], min_val=15, max_val=63)
            select(0, 0)
            columns_read(0)
            pair(0, 0, 1, 0, False)
            with dve.Fori(1, final) as n:
                pair(n, n & 15, (n + 1) & 15, ((n + 1) >> 4) & 3, False)
            pair(final, 15, 0, 0, True)
            dve.wait_ge(scattered, final + 1)
            for b in range(4):
                h = x_sb[:, 2 * b:2 * b + 2, META:ALL]
                V.tensor_tensor(h, h, y_ps[:, 2 * b:2 * b + 2], ALU.add).then_inc(final_ready, 1)


def _chunk_columns():
    q, kv, rq, rv = HEADS * DH, 2 * DH, RH * RDK, RH * RDV
    base = {"q": 0, "k": q, "v": q + kv, "rq": q + 2 * kv}
    base["rk"] = base["rq"] + rq
    base["rv"] = base["rk"] + rq
    base["rg"] = base["rv"] + rv
    base["ga"] = base["rg"] + rv
    base["gr"] = base["ga"] + D
    a = np.arange(DH)

    def columns(kind, i):
        if kind == "q":
            return np.concatenate([i * DH + a, (i + PAIRS) * DH + a])
        return base[kind] + i * P + np.arange(P)
    return columns


def kernel(**inputs):
    import concourse.bacc as bacc
    from concourse.bass_utils import run_bass_kernel_spmd

    a = {k: np.asarray(v) for k, v in inputs.items()}
    h = np.concatenate([a["meta_tokens"], a["x"][0]], 0)
    xT = np.ascontiguousarray(h.T.reshape(KC, P, ALL).transpose(1, 0, 2))
    columns = _chunk_columns()
    w_in = a["w_in"][0]
    rows = np.concatenate([np.concatenate([j * DH + np.arange(DH), (j + PAIRS) * DH + np.arange(DH)])
                           for j in range(PAIRS)])
    full = {"wa": a["w_attn_branch"][0][rows], "wr": a["w_ret_branch"][0], "out": a["w_out"][0]}
    mix_w = np.empty((NU, P, KC, UCOL), np.float32)
    for c, (kind, i) in enumerate(CHUNKS):
        w = full[kind][:, i * P:(i + 1) * P] if kind in full else w_in[:, columns(kind, i)]
        mix_w[c // 2, :, :, (c % 2) * P:(c % 2 + 1) * P] = w.reshape(KC, P, P).transpose(1, 0, 2)
    mix_w = mix_w.reshape(NU, P, KC * UCOL)

    def by_feature(v):
        return v.reshape(KC, P).T

    params = np.concatenate([
        by_feature(a["mix_norm_gain"][0]), by_feature(a["ffn_norm_gain"][0]),
        np.tile(a["q_norm_gain"][0], 2)[:, None], np.tile(a["k_norm_gain"][0], 2)[:, None],
        np.broadcast_to(a["attn_sinks"][0].reshape(2, PAIRS).T.reshape(1, HEADS), (P, HEADS)),
        np.broadcast_to(a["b_router"], (P, EXPERTS)),
        a["w_router"][0].reshape(KC, P, EXPERTS).transpose(1, 0, 2).reshape(P, -1),
        a["b_gate_up"][0].reshape(EXPERTS, 16, P).transpose(2, 0, 1).reshape(P, -1)], 1)
    assert params.shape == (P, N_PARAM)
    arrays = {
        "xT": xT, "mix_w": mix_w, "consts": constants(), "params": np.ascontiguousarray(params),
        "b_down": np.ascontiguousarray(a["b_down"][0]), "w_gate_up": a["w_gate_up"][0], "w_down": a["w_down"][0],
    }
    nc = bacc.Bacc("TRN2", target_bir_lowering=False, num_devices=1)
    args = [nc.dram_tensor(f"in_{k}", v.shape, F32, kind="ExternalInput").ap() for k, v in arrays.items()]
    out = nc.dram_tensor("out", (P, KC, TOK), F32, kind="ExternalOutput").ap()
    build(nc, *args, out)
    r = run_bass_kernel_spmd(nc, [{f"in_{k}": v for k, v in arrays.items()}], core_ids=[0])
    y = np.asarray(r.results[0]["out"])
    return np.ascontiguousarray(y.transpose(2, 1, 0)).reshape(1, TOK, D)
```

```python
from contextlib import ExitStack

import numpy as np

import concourse.bass as bass
from concourse import mybir

F32 = mybir.dt.float32
I32 = mybir.dt.int32
U32 = mybir.dt.uint32
ALU = mybir.AluOpType
ACT = mybir.ActivationFunctionType
AX = mybir.AxisListType

P = 128
D = 1024
KC = D // P
META, TOK = 16, 256
ALL = META + TOK
BLK = 128
HEADS, DH = 16, 64
PAIRS = HEADS // 2
RH, RDK, RDV = 4, 128, 256
EXPERTS, TOPK, FF = 32, 4, 1024
EPS = 1e-5
ALPHA, LIMIT = 1.702, 7.0
SLOTS = 12
UCOL = 256
CAP = 64
B1K, B2K = META + BLK, META + 2 * BLK
SCW = B1K + B2K
MASKED = -1.0e30

UNITS = (["kv"] + ["q"] * 4 + ["rq"] * 2 + ["rk"] * 2 + ["rg"] * 4 + ["ga"] * 2 + ["rv"] * 4
         + ["wa"] * 2 + ["ga", "wa"] * 2 + ["gr", "wr"] * 4 + ["out"] * 4)
NU = len(UNITS)


def chunk_table():
    seen, table = {}, []
    for u in UNITS:
        for half in range(2):
            kind = ("k", "v")[half] if u == "kv" else u
            n = seen.get(kind, 0)
            table.append((kind, n))
            seen[kind] = n + 1
    return table


CHUNKS = chunk_table()
AT = {c: i for i, c in enumerate(CHUNKS)}

CONST_COLS = {}


def _const_layout():
    at = 0
    for name, n in (("ones", P), ("ident", P), ("heads2", P), ("halves", 2), ("eps", 1), ("eps64", 1), ("slopes", 2 * HEADS),
                    ("tri", P), ("iota", TOK), ("alibi", SCW), ("decay", RH * TOK), ("decay_meta", RH * TOK)):
        CONST_COLS[name] = (at, n)
        at += n
    return at


N_CONST = _const_layout()
N_CONST_EARLY = CONST_COLS["tri"][0]

PARAM_COLS = {}


def _param_layout():
    at = 0
    for name, n in (("mix_gain", KC), ("ffn_gain", KC), ("q_gain", 1), ("k_gain", 1), ("sinks", HEADS),
                    ("b_router", EXPERTS), ("w_router", KC * EXPERTS), ("b_gate_up", EXPERTS * 16)):
        PARAM_COLS[name] = (at, n)
        at += n
    return at


N_PARAM = _param_layout()


def constants():
    t = np.zeros((P, N_CONST), np.float64)

    def put(name, a):
        at, n = CONST_COLS[name]
        t[:a.shape[0], at:at + n] = a.reshape(a.shape[0], n)

    p = np.arange(P)
    put("ones", np.ones((P, P)))
    put("ident", np.eye(P))
    put("heads2", (p[:, None] // DH == p[None, :] // DH) * 1.0)
    put("halves", (p[:, None] // DH == np.arange(2)[None]) * 1.0)
    put("eps", np.full((P, 1), EPS))
    put("eps64", np.full((P, 1), DH * EPS))
    slope = 2.0 ** (-8.0 * np.arange(1, HEADS + 1) / HEADS)
    by_pair = np.stack([slope[:PAIRS], slope[PAIRS:]], 1)
    put("slopes", np.broadcast_to(by_pair[None, None], (P, 2, PAIRS, 2)))
    put("tri", (p[:, None] < p[None, :]) * 1.0)
    put("iota", np.broadcast_to(np.arange(TOK)[None], (P, TOK)))
    near = np.where(p[:, None] >= p[None, :], -(p[:, None] - p[None, :]), MASKED)
    far = np.where(p[None, :] > p[:, None], -(BLK + p[:, None] - p[None, :]), MASKED)
    m = np.arange(META)[None]
    put("alibi", np.concatenate([-(META + p[:, None] - m), near, -(META + BLK + p[:, None] - m), far, near], 1))
    gamma = 1.0 - 2.0 ** (-5.0 - np.arange(RH))
    q = np.arange(TOK)
    scale = RDK ** -0.5
    d1 = q[None, :] - p[:, None]
    put("decay", np.where(d1[:, None] >= 0, gamma[None, :, None] ** np.maximum(d1, 0)[:, None], 0.0) * scale)
    dm = META + q[None, :] - np.arange(META)[:, None]
    put("decay_meta", gamma[None, :, None] ** dm[:, None] * scale)
    return t.astype(np.float32)


def build(nc, xT, mix_w, consts, params, b_down, w_gate_up, w_down, out):
    with ExitStack() as ctx:
        def sem(name):
            return ctx.enter_context(nc.semaphore(name))

        ring = ctx.enter_context(nc.sbuf_tensor("ring", [P, SLOTS, 2048], F32))
        arena_bytes = 113280
        arena = ctx.enter_context(nc.sbuf_tensor("arena", [P, arena_bytes // 4], F32))
        cursor = [0]

        def region(cols):
            at = cursor[0]
            cursor[0] += cols
            assert cursor[0] * 4 <= arena_bytes, (cursor[0] * 4, arena_bytes)
            return arena[:, at:at + cols]

        def cut(reg, at, shape, parts=P):
            n = int(np.prod(shape))
            v = reg[0:parts, at:at + n]
            if len(shape) == 2:
                return v.rearrange("p (a b) -> p a b", b=shape[1])
            if len(shape) == 3:
                return v.rearrange("p (a b c) -> p a b c", b=shape[1], c=shape[2])
            return v

        x_sb = cut(region(KC * ALL), 0, (KC, ALL))
        r_u = region(KC * ALL)
        u_sb, u2T = cut(r_u, 0, (KC, ALL)), cut(r_u, 0, (KC, TOK))
        r_q = region(KC * TOK)
        qT, sig_rg, merged = (cut(r_q, 0, (KC, TOK)) for _ in range(3))
        u2tok = cut(r_q, 0, (2, D))
        r_att = region(KC * ALL)
        xsq, attT = cut(r_att, 0, (KC, ALL)), cut(r_att, 0, (PAIRS, TOK))
        e_gate, e_up = (cut(r_att, 1024 * i, (8, 2 * CAP)) for i in range(2))
        r_rg = region(KC * TOK)
        rgT = cut(r_rg, 0, (KC, TOK))
        e_sig, e_act = (cut(r_rg, 1024 * i, (8, 2 * CAP)) for i in range(2))
        r_gate = region(4 * TOK)
        gate_sb, e_out = cut(r_gate, 0, (4, TOK)), cut(r_gate, 0, (D,))
        r_rq = region(RH * TOK + RH * ALL)
        rqT, rkT = cut(r_rq, 0, (RH, TOK)), cut(r_rq, RH * TOK, (RH, ALL))
        xeT = cut(r_rq, 0, (KC, 2 * CAP))
        rt = 1024
        logits, chosen, wgt, posm = (cut(r_rq, rt + 64 * i, (2, EXPERTS)) for i in range(4))
        top8 = cut(r_rq, rt + 256, (2, 8))
        top8i = cut(r_rq, rt + 272, (2, 8)).bitcast(U32)
        top8f = cut(r_rq, rt + 288, (2, 8))
        neg_top, wsum, wrec = (cut(r_rq, rt + 304 + 2 * i, (2,)) for i in range(3))
        n_max, n_over, n_tmp = (cut(r_rq, rt + 310 + i, (1,)) for i in range(3))
        last_pair_i = cut(r_rq, rt + 314, (1,)).bitcast(I32)
        count = cut(r_rq, rt + 316, (EXPERTS,))
        wgtT = cut(r_rq, rt + 352, (TOK,), EXPERTS)
        r_rv = region(3 * D)
        kz = cut(r_rv, 0, (2, ALL))
        vz = cut(r_rv, 2 * ALL, (2, 2, P))
        vz_meta = cut(r_rv, 2 * ALL + 4 * P, (2, P), META)
        rv_tok, rv_meta = cut(r_rv, 0, (2, D)), cut(r_rv, 2 * D, (D,), META)
        hsq = cut(r_rv, 0, (KC, TOK))
        gu_raw = cut(r_rv, 0, (16, P))
        r_p = region(2 * 2 * SCW + 4 * BLK + 6 * BLK)
        prob = cut(r_p, 0, (2, 2, SCW))
        probT_meta = cut(r_p, 4 * SCW, (4, BLK), META)
        probT = cut(r_p, 4 * SCW + 4 * BLK, (6, BLK))
        sel, selw, selwT = cut(r_p, 0, (2, 2 * CAP)), cut(r_p, 256, (2, 2 * CAP)), cut(r_p, 512, (TOK,))
        rs, rs_meta = cut(r_p, 0, (RH, 3 * BLK)), cut(r_p, RH * 3 * BLK, (RH, TOK), META)
        tmp = cut(region(2 * 2 * TOK), 0, (2, 2 * TOK))
        sq = cut(region(2 * 2 * TOK), 0, (2, 2 * TOK))
        r_mix = region(ALL)
        root = region(ALL)
        par = region(N_PARAM)
        b_dn = cut(region(D), 0, (D,), EXPERTS)
        con = region(N_CONST)
        small = region(96)
        q_norm, q_rho, q_slope = (cut(small, 32 * i, (2, PAIRS, 2)) for i in range(3))
        v_tok = region(2)
        soft = region(40)
        s_max, s_neg, s_sink, s_esink, s_sum, s_den, s_rec = (cut(soft, 4 * i, (2, 2)) for i in range(7))

        def const(name, parts=P):
            at, n = CONST_COLS[name]
            return con[0:parts, at:at + n]

        def param(name):
            at, n = PARAM_COLS[name]
            return par[:, at:at + n]

        ones, ident = const("ones"), const("ident")
        decay = const("decay").rearrange("p (h q) -> p h q", h=RH)
        decay_meta = const("decay_meta", META).rearrange("p (h q) -> p h q", h=RH)
        sinks = param("sinks").rearrange("p (j x) -> p j x", x=2)
        w_rt = param("w_router").rearrange("p (k e) -> p k e", k=KC)
        b_gu = param("b_gate_up").rearrange("p (e c) -> p e c", e=EXPERTS)
        slopes = const("slopes").rearrange("p (b j x) -> p b j x", b=2, x=2)

        ps = ctx.enter_context(nc.psum_tensor("ps", [P, 8, 512], F32))
        PROJ, SCORE, PT_META, PT, PV = 0, 2, 4, 5, 7
        COUNT, WT, LOGIT = 0, 1, 3
        GATE, UP, Y = 0, 2, 4
        y_ps = ps[:, Y:Y + 4, :].rearrange("p b (c t) -> p (b c) t", t=TOK)

        landed = [sem(f"landed{i}") for i in range(SLOTS)]
        x_in = [sem("x_in0"), sem("x_in1")]
        early_in, params_in, late_in, bdown_in = sem("early_in"), sem("params_in"), sem("late_in"), sem("bdown_in")
        gained = sem("gained")
        squared = sem("squared")
        mix_stat = sem("mix_stat")
        mix_root = sem("mix_root")
        mix_r = sem("mix_r")
        zeros_set = sem("zeros_set")
        proj_done, proj_read = sem("proj_done"), sem("proj_read")
        k_sq, k_stat, k_root = sem("k_sq"), sem("k_stat"), sem("k_root")
        k_ready, v_turned, v_ready = sem("k_ready"), sem("v_turned"), sem("v_ready")
        q_sq, q_stat, q_root, q_ready = sem("q_sq"), sem("q_stat"), sem("q_root"), sem("q_ready")
        scored, score_read, biased = sem("scored"), sem("score_read"), sem("biased")
        exped, prob_ready = sem("exped"), sem("prob_ready")
        turned, turn_read, att_done, att_read = sem("turned"), sem("turn_read"), sem("att_done"), sem("att_read")
        sig_done = sem("sig_done")
        rv_turned, rv_read = sem("rv_turned"), sem("rv_read")
        rscored, rscore_read = sem("rscored"), sem("rscore_read")
        ret_done, ret_sq, ret_stat, ret_root, ret_ready = (sem("ret_done"), sem("ret_sq"), sem("ret_stat"),
                                                          sem("ret_root"), sem("ret_ready"))
        gate_sig = sem("gate_sig")
        h_sq, h_stat, h_root, u2_ready = sem("h_sq"), sem("h_stat"), sem("h_root"), sem("u2_ready")
        u2_turned, u2tok_ready = sem("u2_turned"), sem("u2tok_ready")
        logit_done, top_ready, route_exp = sem("logit_done"), sem("top_ready"), sem("route_exp")
        chosen_ready, counted, pairs_ready = sem("chosen_ready"), sem("counted"), sem("pairs_ready")
        wgt_ready, wgt_turned, wgtT_ready = sem("wgt_ready"), sem("wgt_turned"), sem("wgtT_ready")
        sel_ready, selw_ready = sem("sel_ready"), sem("selw_ready")
        units_used = sem("units_used")
        gathered, xe_ready = sem("gathered"), sem("xe_ready")
        raw_copied, gu_turned, gate_read = sem("raw_copied"), sem("gu_turned"), sem("gate_read")
        up_biased, gate_ready = sem("up_biased"), sem("gate_ready")
        sig_ready, act_ready, eout_ready = sem("sig_ready"), sem("act_ready"), sem("eout_ready")
        selw_turned, selwT_ready = sem("selw_turned"), sem("selwT_ready")
        scattered, final_ready, stored = sem("scattered"), sem("final_ready"), sem("stored")
        vec_step = sem("vec_step")

        block = ctx.enter_context(nc.Block())

        @block.sync
        def _(sp):
            for h in range(2):
                sp.dma_start(x_sb[:, 4 * h:4 * h + 4], xT[:, 4 * h:4 * h + 4]).then_inc(x_in[h], 16)
            for u in range(NU):
                if u >= SLOTS:
                    sp.wait_ge(proj_done, 2 * (u - SLOTS + 1))
                sp.dma_start(ring[:, u % SLOTS], mix_w[u]).then_inc(landed[u % SLOTS], 16)

            def pair_units(n, lap):
                for q in range(24):
                    j, x = divmod(q, 2)
                    if isinstance(n, int) and n == 0 and q < SLOTS:
                        sp.wait_ge(proj_done, 2 * (NU + q - SLOTS + 1))
                    else:
                        sp.wait_ge(units_used, 24 * n + (q - SLOTS + 1))
                    slot = (NU + q) % SLOTS
                    e = bass.ds(2 * lap + x, 1)
                    if j < 8:
                        dst = ring[:, slot]
                        src = w_gate_up[e, j * P:(j + 1) * P, :].rearrange("o p n -> (o p) n")
                    else:
                        r = 2 * (j - 8) * P
                        dst = ring[:, slot].rearrange("p (c n) -> p c n", c=2)
                        src = w_down[e, r:r + 2 * P, :].rearrange("o (c p) n -> (o p) c n", p=P)
                    sp.dma_start(dst, src).then_inc(landed[slot], 16)

            pair_units(0, 0)
            with sp.Fori(1, 15) as n:
                pair_units(n, n)
            sp.wait_ge(pairs_ready, 1)
            final = sp.value_load(last_pair_i[0:1, :], min_val=15, max_val=63)
            with sp.Fori(15, final + 1) as n:
                lap = sp.compute_val(n & 15)
                pair_units(n, lap)
            for b in range(4):
                sp.wait_ge(final_ready, b + 1)
                sp.dma_start(out[:, 2 * b:2 * b + 2], x_sb[:, 2 * b:2 * b + 2, META:ALL]).then_inc(stored, 16)
            sp.wait_ge(stored, 64)

        @block.gpsimd
        def _(pool):
            empty = (kz[DH:P, 0, :], kz[0:DH, 1, :], vz[:, 0, :, DH:P], vz[:, 1, :, 0:DH],
                     vz_meta[:, 0, DH:P], vz_meta[:, 1, 0:DH])
            for n, v in enumerate(empty):
                if n >= 1:
                    pool.wait_ge(zeros_set, n)
                nc.gpsimd.memset(v, 0.0).then_inc(zeros_set, 1)

        @block.tensor
        def _(pe):
            mm, turn = nc.tensor.matmul, nc.tensor.transpose

            def project(c):
                kind, i = CHUNKS[c]
                unit, half = divmod(c, 2)
                if half == 0:
                    pe.wait_ge(landed[unit % SLOTS], 16 * (unit // SLOTS + 1))
                if c >= 2:
                    pe.wait_ge(proj_read, c - 1)
                if kind == "wa" and i == 0:
                    pe.wait_ge(att_read, PAIRS)
                if kind == "wr" and i == 0:
                    pe.wait_ge(ret_ready, RH)
                if kind == "out" and i == 0:
                    pe.wait_ge(proj_read, c)
                w = ring[:, unit % SLOTS].rearrange("p (k n) -> p k n", k=KC)
                for k in range(KC):
                    if kind == "wa":
                        rhs = attT[:, k]
                    elif kind == "wr":
                        rhs = rgT[:, k]
                    elif kind == "out":
                        rhs = merged[:, k]
                    elif kind in ("k", "v", "rk", "rv"):
                        rhs = u_sb[:, k]
                    else:
                        rhs = u_sb[:, k, META:ALL]
                    last = mm(ps[:, PROJ + half, 0:rhs.shape[-1]], w[:, k, half * P:(half + 1) * P], rhs,
                              start=(k == 0), stop=(k == KC - 1))
                last.then_inc(proj_done, 1)

            def mix_stats():
                for k in range(KC):
                    if k % 4 == 0:
                        pe.wait_ge(squared, k // 4 + 1)
                    last = mm(ps[:, SCORE, 0:ALL], ones, xsq[:, k], start=(k == 0), stop=(k == KC - 1))
                last.then_inc(mix_stat, 1)
                for b in range(2):
                    for k in range(KC):
                        last = mm(ps[:, PV, 32 + b:33 + b], xsq[:, k, META + b * BLK:META + (b + 1) * BLK],
                                  ones[:, 0:1], start=(k == 0), stop=(k == KC - 1))
                last.then_inc(mix_stat, 1)

            def q_stats(j):
                pe.wait_ge(q_sq, j + 1)
                for b in range(2):
                    at = b * HEADS + 2 * j
                    last = mm(ps[:, PV, at:at + 2], sq[:, j % 2, b * BLK:(b + 1) * BLK], const("halves"),
                              start=True, stop=True)
                last.then_inc(q_stat, 1)

            def scores(j):
                if j == 0:
                    pe.wait_ge(q_ready, 1)
                    pe.wait_ge(k_ready, 2)
                    pe.wait_ge(zeros_set, 6)
                else:
                    pe.wait_ge(score_read, j)
                for x in range(2):
                    mm(ps[:, SCORE + x, 0:B1K], qT[:, j, 0:BLK], kz[:, x, 0:B1K], start=True, stop=True)
                    last = mm(ps[:, SCORE + x, B1K:SCW], qT[:, j, BLK:TOK], kz[:, x, :], start=True, stop=True)
                last.then_inc(scored, 1)

            def turn_probs(j):
                pe.wait_ge(prob_ready, j + 1)
                if j >= 1:
                    pe.wait_ge(turn_read, j)
                for x in range(2):
                    p_x = prob[:, j % 2, x]
                    for b, at in ((0, 0), (1, B1K)):
                        turn(ps[0:META, PT_META, (2 * b + x) * BLK:(2 * b + x + 1) * BLK], p_x[:, at:at + META], ident)
                    for c, at in enumerate((META, B1K + META, B1K + META + BLK)):
                        last = turn(ps[:, PT + x, c * BLK:(c + 1) * BLK], p_x[:, at:at + BLK], ident)
                last.then_inc(turned, 1)

            def attend(j):
                if j == 0:
                    pe.wait_ge(v_ready, 4)
                    pe.wait_ge(q_root, 2)
                else:
                    pe.wait_ge(att_read, j)
                pe.wait_ge(turn_read, j + 1)
                for b in range(2):
                    o = ps[:, PV, b * BLK:(b + 1) * BLK]
                    for x in range(2):
                        mm(o, vz_meta[:, x], probT_meta[:, 2 * b + x], start=(x == 0), stop=False)
                        for c in range(b + 1):
                            last = mm(o, vz[:, x, c], probT[:, 3 * x + b + c], start=False, stop=(x == 1 and c == b))
                last.then_inc(att_done, 1)

            def turn_value(i):
                bank = PT_META + i % 2
                pe.wait_ge(proj_read, AT[("rv", i)] + 1)
                if i >= 2:
                    pe.wait_ge(rv_read, i - 1)
                t = tmp[:, i % 2]
                turn(ps[0:META, bank, 0:P], t[:, 0:META], ident)
                turn(ps[:, bank, P:2 * P], t[:, META:META + BLK], ident)
                turn(ps[:, bank, 2 * P:3 * P], t[:, META + BLK:ALL], ident).then_inc(rv_turned, 1)

            def ret_scores(h):
                if h == 0:
                    pe.wait_ge(score_read, PAIRS)
                else:
                    pe.wait_ge(rscore_read, h)
                q = rqT[:, h]
                mm(ps[:, SCORE, 0:TOK], rkT[:, h, META:META + BLK], q, start=True, stop=True)
                mm(ps[:, SCORE, TOK:TOK + BLK], rkT[:, h, META + BLK:ALL], q[:, BLK:TOK], start=True, stop=True)
                mm(ps[0:META, SCORE + 1, 0:TOK], rkT[:, h, 0:META], q, start=True, stop=True).then_inc(rscored, 1)

            def ret_bank(h):
                return (SCORE, SCORE + 1, PT + 1, PV)[h]

            def retain(h):
                pe.wait_ge(rscore_read, RH)
                pe.wait_ge(rv_read, 2 * RH)
                bank = ret_bank(h)
                for v in range(2):
                    f = slice((2 * h + v) * P, (2 * h + v + 1) * P)
                    o = ps[:, bank, v * TOK:(v + 1) * TOK]
                    mm(o, rv_meta[:, f], rs_meta[:, h], start=True, stop=False, skip_group_check=True)
                    mm(o, rv_tok[:, 0, f], rs[:, h, 0:TOK], start=False, stop=False, skip_group_check=True)
                    last = mm(o[:, BLK:TOK], rv_tok[:, 1, f], rs[:, h, TOK:TOK + BLK], start=False, stop=True,
                              skip_group_check=True)
                last.then_inc(ret_done, 1)

            def ret_stats(h):
                pe.wait_ge(ret_sq, h + 1)
                bank = PT_META + h % 2
                if h >= 2:
                    pe.wait_ge(ret_root, h - 1)
                for v in range(2):
                    last = mm(ps[:, bank, 0:TOK], ones, sq[:, h % 2, v * TOK:(v + 1) * TOK], start=(v == 0), stop=(v == 1))
                last.then_inc(ret_stat, 1)

            pe.wait_ge(early_in, 16)
            mix_stats()
            pe.wait_ge(gained, 2)
            project(0)
            project(1)
            project(2)
            pe.wait_ge(k_sq, 1)
            mm(ps[:, PT + 1, 0:ALL], const("heads2"), sq[:, 0, 0:ALL], start=True, stop=True).then_inc(k_stat, 1)
            pe.wait_ge(proj_read, AT[("v", 0)] + 1)
            turn(ps[0:META, PT_META, 0:P], tmp[:, 1, 0:META], ident)
            turn(ps[:, PT, 0:P], tmp[:, 1, META:META + BLK], ident)
            turn(ps[:, PT, P:2 * P], tmp[:, 1, META + BLK:ALL], ident).then_inc(v_turned, 1)
            for j in range(PAIRS):
                project(AT[("q", j)] + 1)
                q_stats(j)
            for i in range(PAIRS + 1):
                c = AT[("rq", 0)] + 2 * i
                if i > 0:
                    project(c)
                    turn_probs(i - 1)
                if i < PAIRS:
                    scores(i)
                project(c + 1)
                if i > 0:
                    attend(i - 1)
            project(AT[("ga", 2)])
            project(AT[("ga", 3)])
            for h in range(RH):
                project(AT[("rv", 2 * h)])
                if h > 0:
                    turn_value(2 * h - 1)
                ret_scores(h)
                project(AT[("rv", 2 * h + 1)])
                turn_value(2 * h)
            project(AT[("wa", 0)])
            turn_value(2 * RH - 1)
            project(AT[("wa", 1)])
            retain(0)
            retain(1)
            project(AT[("wa", 2)])
            ret_stats(0)
            retain(2)
            project(AT[("wa", 3)])
            ret_stats(1)
            retain(3)
            project(AT[("ga", 4)])
            ret_stats(2)
            project(AT[("ga", 5)])
            ret_stats(3)
            for c in range(AT[("ga", 5)] + 1, len(CHUNKS)):
                project(c)

            for k in range(KC):
                pe.wait_ge(h_sq, k + 1)
                last = mm(ps[:, SCORE, 0:TOK], ones, hsq[:, k], start=(k == 0), stop=(k == KC - 1))
            last.then_inc(h_stat, 1)
            pe.wait_ge(u2_ready, KC)
            for t in range(2):
                for k in range(KC):
                    last = mm(ps[:, LOGIT, t * EXPERTS:(t + 1) * EXPERTS], u2T[:, k, t * P:(t + 1) * P], w_rt[:, k],
                              start=(k == 0), stop=(k == KC - 1))
            last.then_inc(logit_done, 1)
            for t in range(2):
                for k in range(KC):
                    last = turn(ps[:, Y + 2 * t + k // 4, (k % 4) * P:(k % 4 + 1) * P], u2T[:, k, t * P:(t + 1) * P], ident)
                last.then_inc(u2_turned, 1)
            pe.wait_ge(chosen_ready, 1)
            mm(ps[:, COUNT, 0:EXPERTS], const("tri"), chosen[:, 0], start=True, stop=True)
            mm(ps[:, COUNT, EXPERTS:2 * EXPERTS], ones, chosen[:, 0], start=True, stop=False)
            mm(ps[:, COUNT, EXPERTS:2 * EXPERTS], const("tri"), chosen[:, 1], start=False, stop=True)
            mm(ps[:, COUNT, 2 * EXPERTS:3 * EXPERTS], ones, chosen[:, 0], start=True, stop=False)
            mm(ps[:, COUNT, 2 * EXPERTS:3 * EXPERTS], ones, chosen[:, 1], start=False, stop=True).then_inc(counted, 1)
            pe.wait_ge(wgt_ready, 1)
            for t in range(2):
                last = turn(ps[0:EXPERTS, WT, t * P:(t + 1) * P], wgt[:, t], ident)
            last.then_inc(wgt_turned, 1)
            pe.wait_ge(wgtT_ready, 1)
            pe.wait_ge(bdown_in, 16)
            pe.wait_ge(u2tok_ready, 2)
            for c in range(KC):
                mm(y_ps[:, c], b_dn[:, c * P:(c + 1) * P], wgtT, start=(c % 2 == 0), stop=False, skip_group_check=True)

            def gather():
                for k in range(KC):
                    o = ps[:, GATE + k // 4, (k % 4) * P:(k % 4 + 1) * P]
                    for t in range(2):
                        last = mm(o, u2tok[:, t, k * P:(k + 1) * P], sel[:, t], start=(t == 0), stop=(t == 1))
                last.then_inc(gathered, 1)

            def unit_landed(n, q):
                slot = (NU + q) % SLOTS
                pe.wait_ge(landed[slot], 32 * n + 16 * ((NU + q) // SLOTS + 1))
                return ring[:, slot]

            def gate_up(n):
                pe.wait_ge(xe_ready, n + 1)
                if not (isinstance(n, int) and n == 0):
                    pe.wait_ge(eout_ready, n)
                    pe.wait_ge(selwT_ready, n)
                for q in range(16):
                    j, x = divmod(q, 2)
                    w, half = unit_landed(n, q), slice(x * CAP, (x + 1) * CAP)
                    for b in range(4):
                        last = mm(ps[half, GATE + b], xeT[:, j, half], w[:, b * 512:(b + 1) * 512],
                                  start=(j == 0), stop=(j == 7))
                    last.then_inc(units_used, 1)

            def turn_hidden(n):
                pe.wait_ge(raw_copied, 2 * n + 2)
                for c in range(16):
                    last = turn(ps[:, GATE + c // 4, (c % 4) * P:(c % 4 + 1) * P], gu_raw[:, c], ident)
                last.then_inc(gu_turned, 1)

            def down(n):
                pe.wait_ge(act_ready, n + 1)
                for q in range(16, 24):
                    j, x = divmod(q, 2)
                    w, half = unit_landed(n, q), slice(x * CAP, (x + 1) * CAP)
                    for f in range(2):
                        k = 2 * (j - 8) + f
                        for b in range(2):
                            last = mm(ps[half, UP + b], e_act[:, k, half],
                                      w[:, f * D + b * 512:f * D + (b + 1) * 512], start=(k == 0), stop=(k == 7))
                    last.then_inc(units_used, 1)

            def add_back(c0, c1):
                for c in range(c0, c1):
                    last = mm(y_ps[:, c], e_out[:, c * P:(c + 1) * P], selwT, start=False, stop=False,
                              skip_group_check=True)
                if c1 == KC:
                    last.then_inc(scattered, 1)

            def pair(n, first, last_pair):
                gate_up(n)
                if not first:
                    add_back(0, 4)
                turn_hidden(n)
                if not first:
                    add_back(4, KC)
                if not last_pair:
                    pe.wait_ge(sel_ready, n + 2)
                    pe.wait_ge(gate_read, n + 1)
                    gather()
                down(n)
                pe.wait_ge(selw_ready, n + 1)
                if not last_pair:
                    pe.wait_ge(xe_ready, n + 2)
                for t in range(2):
                    last = turn(ps[:, GATE, t * P:(t + 1) * P], selw[:, t], ident)
                last.then_inc(selw_turned, 1)

            pe.wait_ge(pairs_ready, 1)
            final = pe.value_load(last_pair_i[0:1, :], min_val=15, max_val=63)
            pe.wait_ge(sel_ready, 1)
            gather()
            pair(0, True, False)
            with pe.Fori(1, final) as n:
                pair(n, False, False)
            pair(final, False, True)
            pe.wait_ge(eout_ready, final + 1)
            pe.wait_ge(selwT_ready, final + 1)
            add_back(0, KC)

        @block.scalar
        def _(act):
            A = nc.scalar.activation
            act.dma_start(con[:, 0:N_CONST_EARLY], consts[:, 0:N_CONST_EARLY]).then_inc(early_in, 16)
            act.dma_start(par, params).then_inc(params_in, 16)
            act.dma_start(con[:, N_CONST_EARLY:N_CONST], consts[:, N_CONST_EARLY:N_CONST]).then_inc(late_in, 16)
            act.dma_start(b_dn, b_down).then_inc(bdown_in, 16)
            for h in range(2):
                act.wait_ge(x_in[h], 16)
                A(xsq[:, 4 * h:4 * h + 4], x_sb[:, 4 * h:4 * h + 4], ACT.Square).then_inc(squared, 1)
            act.wait_ge(early_in, 16)
            act.wait_ge(mix_stat, 2)
            A(root, ps[:, SCORE, 0:ALL], ACT.Sqrt, bias=const("eps"), scale=1.0 / D).then_inc(mix_root, 1)
            A(v_tok, ps[:, PV, 32:34], ACT.Copy, scale=1.0 / D).then_inc(mix_root, 1)
            act.wait_ge(params_in, 16)
            act.wait_ge(proj_read, 1)
            A(sq[:, 0, 0:ALL], tmp[:, 0, 0:ALL], ACT.Square).then_inc(k_sq, 1)

            def query(j):
                c = AT[("q", j)]
                act.wait_ge(proj_done, c + 1)
                if j >= 2:
                    act.wait_ge(q_stat, j - 1)
                if j == 0:
                    act.wait_ge(k_stat, 1)
                A(sq[:, j % 2, 0:TOK], ps[:, PROJ + c % 2, 0:TOK], ACT.Square).then_inc(q_sq, 1)
                act.wait_ge(proj_read, c)
                A(qT[:, j], ps[:, PROJ + c % 2, 0:TOK], ACT.Copy, scale=param("q_gain")).then_inc(proj_read, 1)

            query(0)
            act.wait_ge(mix_r, 1)
            A(root, ps[:, PT + 1, 0:ALL], ACT.Sqrt, bias=const("eps"), scale=1.0 / DH).then_inc(k_root, 1)
            act.wait_ge(v_turned, 1)
            act.wait_ge(zeros_set, 6)
            for x in range(2):
                f = slice(x * DH, (x + 1) * DH)
                A(vz_meta[:, x, f], ps[0:META, PT_META, f], ACT.Copy).then_inc(v_ready, 1)
                A(vz[:, x, :, f], ps[:, PT, 0:2 * P].rearrange("p (c f) -> p c f", c=2)[:, :, f],
                  ACT.Copy).then_inc(v_ready, 1)
            for j in range(1, PAIRS):
                query(j)
            act.wait_ge(q_stat, PAIRS)
            act.wait_ge(mix_r, 2)
            for b in range(2):
                A(q_norm[:, b], ps[:, PV, b * HEADS:(b + 1) * HEADS].rearrange("p (j x) -> p j x", x=2), ACT.Sqrt,
                  bias=v_tok[:, b:b + 1]).then_inc(q_root, 1)

            for i in range(PAIRS + 1):
                if i > 0:
                    j = i - 1
                    act.wait_ge(turned, j + 1)
                    if j >= 1:
                        act.wait_ge(att_done, j)
                    A(probT_meta, ps[0:META, PT_META].rearrange("p (a b) -> p a b", b=BLK), ACT.Copy)
                    A(probT.rearrange("p (x c) q -> p x (c q)", x=2), ps[:, PT:PT + 2, 0:3 * BLK],
                      ACT.Copy).then_inc(turn_read, 1)
                if i < PAIRS:
                    act.wait_ge(biased, i + 1)
                    for x in range(2):
                        for b, (lo, hi) in enumerate(((0, B1K), (B1K, SCW))):
                            v = prob[:, i % 2, x, lo:hi]
                            A(v, v, ACT.Exp, bias=s_neg[:, b, x:x + 1], scale=q_rho[:, b, i, x:x + 1],
                              accum_out=s_sum[:, b, x:x + 1])
                    A(s_esink, s_sink, ACT.Exp).then_inc(exped, 1)
                if i > 0:
                    act.wait_ge(att_done, i)
                    A(attT[:, i - 1], ps[:, PV, 0:TOK], ACT.Copy).then_inc(att_read, 1)

            act.wait_ge(proj_read, AT[("ga", 3)] + 1)
            for h in range(RH):
                A(sig_rg[:, 2 * h:2 * h + 2], rgT[:, 2 * h:2 * h + 2], ACT.Sigmoid).then_inc(sig_done, 1)
            A(gate_sb, gate_sb, ACT.Sigmoid).then_inc(gate_sig, 4)

            def value_read(i):
                act.wait_ge(rv_turned, i + 1)
                bank = PT_META + i % 2
                f = slice(i * P, (i + 1) * P)
                A(rv_meta[:, f], ps[0:META, bank, 0:P], ACT.Copy)
                A(rv_tok[:, :, f], ps[:, bank, P:3 * P].rearrange("p (c f) -> p c f", c=2), ACT.Copy).then_inc(rv_read, 1)

            for i in range(2 * RH):
                value_read(i)

            def ret_bank(h):
                return (SCORE, SCORE + 1, PT + 1, PV)[h]

            def ret_square(h):
                act.wait_ge(ret_done, h + 1)
                if h >= 2:
                    act.wait_ge(ret_stat, h - 1)
                A(sq[:, h % 2], ps[:, ret_bank(h)], ACT.Square).then_inc(ret_sq, 1)

            def ret_sqrt(h):
                act.wait_ge(ret_stat, h + 1)
                if h >= 1:
                    act.wait_ge(ret_ready, h)
                A(root[:, 0:TOK], ps[:, PT_META + h % 2, 0:TOK], ACT.Sqrt, bias=const("eps"),
                  scale=1.0 / RDV).then_inc(ret_root, 1)

            ret_square(0)
            ret_square(1)
            ret_sqrt(0)
            ret_square(2)
            ret_sqrt(1)
            ret_square(3)
            ret_sqrt(2)
            ret_sqrt(3)
            for kind in ("ga", "gr"):
                for i in range(4 if kind == "ga" else 0, KC):
                    act.wait_ge(proj_read, AT[(kind, i)] + 1)
                    A(gate_sb[:, i % 4], gate_sb[:, i % 4], ACT.Sigmoid).then_inc(gate_sig, 1)
            for k in range(KC):
                act.wait_ge(proj_read, AT[("out", k)] + 1)
                A(hsq[:, k], x_sb[:, k, META:ALL], ACT.Square).then_inc(h_sq, 1)
            act.wait_ge(h_stat, 1)
            A(root[:, 0:TOK], ps[:, SCORE, 0:TOK], ACT.Sqrt, bias=const("eps"), scale=1.0 / D).then_inc(h_root, 1)
            for t in range(2):
                act.wait_ge(u2_turned, t + 1)
                A(u2tok[:, t].rearrange("p (b f) -> p b f", b=2), ps[:, Y + 2 * t:Y + 2 * t + 2], ACT.Copy).then_inc(u2tok_ready, 1)
            act.wait_ge(top_ready, 1)
            for t in range(2):
                A(wgt[:, t], logits[:, t], ACT.Exp, bias=neg_top[:, t:t + 1]).then_inc(route_exp, 1)
            act.wait_ge(wgt_turned, 1)
            A(wgtT, ps[0:EXPERTS, WT, 0:TOK], ACT.Copy).then_inc(wgtT_ready, 1)

            def pair(n):
                act.wait_ge(units_used, 24 * n + 16)
                A(gu_raw[:, 0:8].rearrange("p (b c) f -> p b (c f)", b=2), ps[:, GATE:GATE + 2],
                  ACT.Copy).then_inc(raw_copied, 1)
                act.wait_ge(gate_ready, n + 1)
                A(e_sig, e_gate, ACT.Sigmoid, scale=ALPHA).then_inc(sig_ready, 1)
                act.wait_ge(units_used, 24 * n + 24)
                A(e_out.rearrange("p (b f) -> p b f", b=2), ps[:, UP:UP + 2], ACT.Copy).then_inc(eout_ready, 1)
                act.wait_ge(selw_turned, n + 1)
                A(selwT, ps[:, GATE, 0:TOK], ACT.Copy).then_inc(selwT_ready, 1)

            act.wait_ge(pairs_ready, 1)
            final = act.value_load(last_pair_i[0:1, :], min_val=15, max_val=63)
            with act.Fori(0, final + 1) as n:
                pair(n)

        @block.vector
        def _(dve):
            V = nc.vector
            steps = [0]

            def link(ins):
                steps[0] += 1
                ins.then_inc(vec_step, 1)
                dve.wait_ge(vec_step, steps[0])

            dve.wait_ge(params_in, 16)
            for h in range(2):
                dve.wait_ge(x_in[h], 16)
                for k in range(4 * h, 4 * h + 4):
                    last = V.tensor_scalar(u_sb[:, k], x_sb[:, k], param("mix_gain")[:, k:k + 1], None, ALU.mult)
                last.then_inc(gained, 1)
            dve.wait_ge(mix_root, 2)
            V.reciprocal(r_mix, root).then_inc(mix_r, 1)
            V.tensor_scalar(v_tok, v_tok, EPS, DH * EPS, ALU.add, ALU.mult).then_inc(mix_r, 1)
            dve.wait_ge(mix_r, 2)

            def evict(c, dst):
                n = dst.shape[-1]
                dve.wait_ge(proj_done, c + 1)
                V.tensor_tensor(dst, ps[:, PROJ + c % 2, 0:n], r_mix[:, ALL - n:ALL], ALU.mult).then_inc(proj_read, 1)

            evict(0, tmp[:, 0, 0:ALL])
            evict(1, tmp[:, 1, 0:ALL])
            dve.wait_ge(k_root, 1)
            dve.wait_ge(proj_read, 2)
            link(V.reciprocal(root, root))
            dve.wait_ge(zeros_set, 6)
            for x in range(2):
                f = slice(x * DH, (x + 1) * DH)
                V.scalar_tensor_tensor(kz[f, x], tmp[f, 0, 0:ALL], param("k_gain")[f], root[f], ALU.mult,
                                       ALU.mult).then_inc(k_ready, 1)
            dve.wait_ge(q_root, 2)
            V.reciprocal(q_rho, q_norm).then_inc(q_ready, 1)
            dve.wait_ge(late_in, 16)
            link(V.tensor_tensor(q_slope, q_norm, slopes, ALU.mult))

            def place_of(c):
                kind, i = CHUNKS[c]
                return {"rq": rqT, "rk": rkT, "rg": rgT, "ga": gate_sb}[kind][:, i]

            def bias_scores(i):
                dve.wait_ge(scored, i + 1)
                for x in range(2):
                    for b, (lo, hi) in enumerate(((0, B1K), (B1K, SCW))):
                        last = V.scalar_tensor_tensor(prob[:, i % 2, x, lo:hi], const("alibi")[:, lo:hi],
                                                      q_slope[:, b, i, x:x + 1], ps[:, SCORE + x, lo:hi],
                                                      ALU.mult, ALU.add)
                last.then_inc(score_read, 1)
                dve.wait_ge(score_read, i + 1)
                V.tensor_reduce(s_max[:, 0], prob[:, i % 2, :, 0:B1K], AX.X, ALU.max)
                link(V.tensor_reduce(s_max[:, 1], prob[:, i % 2, :, B1K:SCW], AX.X, ALU.max))
                link(V.tensor_tensor(s_max, s_max, q_rho[:, :, i], ALU.mult))
                sink = sinks[:, i:i + 1].to_broadcast([P, 2, 2])
                link(V.tensor_tensor(s_max, s_max, sink, ALU.max))
                if i >= 1:
                    dve.wait_ge(exped, i)
                V.tensor_scalar(s_neg, s_max, -1.0, None, ALU.mult)
                V.tensor_tensor(s_sink, sink, s_max, ALU.subtract).then_inc(biased, 1)

            def normalise(i):
                dve.wait_ge(exped, i + 1)
                link(V.tensor_tensor(s_den, s_sum, s_esink, ALU.add))
                link(V.reciprocal(s_rec, s_den))
                for x in range(2):
                    for b, (lo, hi) in enumerate(((0, B1K), (B1K, SCW))):
                        v = prob[:, i % 2, x, lo:hi]
                        last = V.tensor_scalar(v, v, s_rec[:, b, x:x + 1], None, ALU.mult)
                last.then_inc(prob_ready, 1)

            evict_first = AT[("rq", 0)]
            dve.wait_ge(proj_read, evict_first)
            for i in range(PAIRS + 1):
                c = AT[("rq", 0)] + 2 * i
                evict(c, place_of(c))
                if i < PAIRS:
                    bias_scores(i)
                evict(c + 1, place_of(c + 1))
                if i < PAIRS:
                    normalise(i)
            evict(AT[("ga", 2)], gate_sb[:, 2])
            evict(AT[("ga", 3)], gate_sb[:, 3])
            for h in range(RH):
                for v in range(2):
                    i = 2 * h + v
                    if i >= 2:
                        dve.wait_ge(rv_turned, i - 1)
                    if i == 0:
                        dve.wait_ge(att_done, PAIRS)
                    evict(AT[("rv", i)], tmp[:, i % 2, 0:ALL])
                    if v == 0:
                        dve.wait_ge(rscored, h + 1)
                        V.tensor_tensor(rs[:, h, 0:TOK], ps[:, SCORE, 0:TOK], decay[:, h], ALU.mult)
                        V.tensor_tensor(rs[:, h, TOK:TOK + BLK], ps[:, SCORE, TOK:TOK + BLK], decay[:, h, 0:BLK], ALU.mult)
                        V.tensor_tensor(rs_meta[:, h], ps[0:META, SCORE + 1, 0:TOK], decay_meta[:, h],
                                        ALU.mult).then_inc(rscore_read, 1)
                dve.wait_ge(sig_done, h + 1)
                link(V.tensor_tensor(rgT[:, 2 * h:2 * h + 2], rgT[:, 2 * h:2 * h + 2], sig_rg[:, 2 * h:2 * h + 2], ALU.mult))

            def ret_out(h):
                bank = (SCORE, SCORE + 1, PT + 1, PV)[h]
                dve.wait_ge(ret_root, h + 1)
                rr = tmp[:, 0, 0:TOK]
                link(V.reciprocal(rr, root[:, 0:TOK]))
                g = rgT[:, 2 * h:2 * h + 2]
                link(V.tensor_tensor(g, g, rr.rearrange("p (o t) -> p o t", o=1).to_broadcast([P, 2, TOK]), ALU.mult))
                V.tensor_tensor(g, g, ps[:, bank].rearrange("p (v t) -> p v t", v=2), ALU.mult).then_inc(ret_ready, 1)

            def merge(c):
                kind, i = CHUNKS[c]
                b = ps[:, PROJ + c % 2, 0:TOK]
                if kind in ("ga", "gr"):
                    if i >= 4 or kind == "gr":
                        evict(c, gate_sb[:, i % 4])
                elif kind == "wa":
                    dve.wait_ge(gate_sig, i + 1)
                    dve.wait_ge(proj_done, c + 1)
                    V.tensor_tensor(merged[:, i], b, gate_sb[:, i % 4], ALU.mult).then_inc(proj_read, 1)
                elif kind == "wr":
                    dve.wait_ge(gate_sig, KC + i + 1)
                    dve.wait_ge(proj_done, c + 1)
                    gated = tmp[:, (i + 1) % 2, 0:TOK]
                    link(V.tensor_tensor(gated, b, gate_sb[:, i % 4], ALU.mult))
                    V.tensor_tensor(merged[:, i], merged[:, i], gated, ALU.add).then_inc(proj_read, 1)
                elif kind == "out":
                    dve.wait_ge(proj_done, c + 1)
                    h = x_sb[:, i, META:ALL]
                    V.tensor_tensor(h, h, b, ALU.add).then_inc(proj_read, 1)

            for c in range(AT[("wa", 0)], len(CHUNKS)):
                merge(c)
                if c == AT[("wa", 3)]:
                    ret_out(0)
                if c == AT[("ga", 4)]:
                    ret_out(1)
                if c == AT[("ga", 5)]:
                    ret_out(2)
                if c == AT[("ga", 5)] + 1:
                    ret_out(3)

            dve.wait_ge(h_root, 1)
            dve.wait_ge(proj_read, len(CHUNKS))
            r2 = tmp[:, 0, 0:TOK]
            link(V.reciprocal(r2, root[:, 0:TOK]))
            for k in range(KC):
                V.scalar_tensor_tensor(u2T[:, k], x_sb[:, k, META:ALL], param("ffn_gain")[:, k:k + 1], r2, ALU.mult,
                                       ALU.mult).then_inc(u2_ready, 1)
            dve.wait_ge(logit_done, 1)
            br = param("b_router").rearrange("p (o e) -> p o e", o=1).to_broadcast([P, 2, EXPERTS])
            link(V.tensor_tensor(logits, ps[:, LOGIT, 0:2 * EXPERTS].rearrange("p (t e) -> p t e", t=2), br, ALU.add))
            for t in range(2):
                link(V.max(top8[:, t], logits[:, t]))
            V.tensor_scalar(neg_top, top8[:, :, 0], -1.0, None, ALU.mult).then_inc(top_ready, 1)
            for t in range(2):
                link(V.max_index(top8i[:, t], top8[:, t], logits[:, t]))
            link(V.tensor_copy(top8f, top8i))
            i32 = const("iota")[:, 0:EXPERTS]
            for t in range(2):
                link(V.tensor_scalar(chosen[:, t], i32, top8f[:, t, 0:1], None, ALU.is_equal))
                for r in range(1, TOPK):
                    ins = V.scalar_tensor_tensor(chosen[:, t], i32, top8f[:, t, r:r + 1], chosen[:, t], ALU.is_equal, ALU.add)
                    if t == 1 and r == TOPK - 1:
                        ins.then_inc(chosen_ready, 1)
                        dve.wait_ge(chosen_ready, 1)
                    else:
                        link(ins)
            dve.wait_ge(route_exp, 2)
            link(V.tensor_tensor(wgt, wgt, chosen, ALU.mult))
            link(V.tensor_reduce(wsum, wgt, AX.X, ALU.add))
            link(V.reciprocal(wrec, wsum))
            V.tensor_scalar(wgt[:, 0], wgt[:, 0], wrec[:, 0:1], None, ALU.mult)
            V.tensor_scalar(wgt[:, 1], wgt[:, 1], wrec[:, 1:2], None, ALU.mult).then_inc(wgt_ready, 1)
            dve.wait_ge(counted, 1)
            pos = ps[:, COUNT, 0:2 * EXPERTS].rearrange("p (t e) -> p t e", t=2)
            link(V.scalar_tensor_tensor(posm, pos, 1.0, chosen, ALU.add, ALU.mult))
            link(V.tensor_scalar(posm, posm, -1.0, None, ALU.add))
            link(V.tensor_copy(count, ps[:, COUNT, 2 * EXPERTS:3 * EXPERTS]))
            link(V.tensor_reduce(n_max, count, AX.X, ALU.max))
            link(V.tensor_scalar(n_over, n_max, float(CAP), 16.0, ALU.is_gt, ALU.mult))
            for r in (2, 3):
                link(V.tensor_scalar(n_tmp, n_max, float(r * CAP), 16.0, ALU.is_gt, ALU.mult))
                link(V.tensor_tensor(n_over, n_over, n_tmp, ALU.add))
            V.tensor_scalar(last_pair_i, n_over, 15.0, None, ALU.add).then_inc(pairs_ready, 1)

            def select(lap, rnd):
                place = posm[:, :, bass.ds(2 * lap, 2)]
                col = const("iota")[:, bass.ds(CAP * rnd, CAP)]
                V.tensor_tensor(sel.rearrange("p t (x s) -> p t x s", x=2),
                                col.rearrange("p (a b s) -> p a b s", a=1, b=1).to_broadcast([P, 2, 2, CAP]),
                                place.rearrange("p t (x o) -> p t x o", o=1).to_broadcast([P, 2, 2, CAP]),
                                ALU.is_equal).then_inc(sel_ready, 1)

            def weigh(n, lap):
                w = wgt[:, :, bass.ds(2 * lap, 2)]
                dve.wait_ge(sel_ready, n + 1)
                V.tensor_tensor(selw.rearrange("p t (x s) -> p t x s", x=2), sel.rearrange("p t (x s) -> p t x s", x=2),
                                w.rearrange("p t (x o) -> p t x o", o=1).to_broadcast([P, 2, 2, CAP]),
                                ALU.mult).then_inc(selw_ready, 1)

            def columns_read(n):
                dve.wait_ge(gathered, n + 1)
                V.tensor_copy(xeT.rearrange("p (b c) s -> p b (c s)", b=2), ps[:, GATE:GATE + 2]).then_inc(xe_ready, 1)

            def hidden(n, lap):
                def link(ins, k):
                    ins.then_inc(vec_step, 1)
                    dve.wait_ge(vec_step, 2 * n + step0 + k)

                def biased(out, bank, half, sem_read, sem_value):
                    for b in range(2):
                        at = 8 * half + 4 * b
                        bias = b_gu[:, bass.ds(2 * lap, 2), at:at + 4].rearrange("p x (k s) -> p k x s", s=1)
                        last = V.tensor_tensor(out[:, 4 * b:4 * b + 4].rearrange("p k (x s) -> p k x s", x=2),
                                               ps[:, bank + b].rearrange("p (k x s) -> p k x s", k=4, x=2),
                                               bias.to_broadcast([P, 4, 2, CAP]), ALU.add)
                    last.then_inc(sem_read, 1)
                    dve.wait_ge(sem_read, sem_value)

                dve.wait_ge(units_used, 24 * n + 16)
                V.tensor_copy(gu_raw[:, 8:16].rearrange("p (b c) f -> p b (c f)", b=2),
                              ps[:, UP:UP + 2]).then_inc(raw_copied, 1)
                dve.wait_ge(gu_turned, n + 1)
                biased(e_gate, GATE, 0, gate_read, n + 1)
                V.tensor_scalar(e_gate, e_gate, LIMIT, None, ALU.min).then_inc(gate_ready, 1)
                biased(e_up, UP, 1, up_biased, n + 1)
                link(V.tensor_scalar(e_up, e_up, LIMIT, -LIMIT, ALU.min, ALU.max), 1)
                link(V.scalar_tensor_tensor(e_up, e_up, 1.0, e_gate, ALU.add, ALU.mult), 2)
                dve.wait_ge(sig_ready, n + 1)
                V.tensor_tensor(e_act, e_up, e_sig, ALU.mult).then_inc(act_ready, 1)

            step0 = steps[0]

            def pair(n, lap, next_lap, next_rnd, first, last_pair):
                if not first:
                    dve.wait_ge(selw_turned, n)
                weigh(n, lap)
                if not last_pair:
                    dve.wait_ge(selw_ready, n + 1)
                    select(next_lap, next_rnd)
                hidden(n, lap)
                if not last_pair:
                    columns_read(n + 1)

            dve.wait_ge(pairs_ready, 1)
            final = dve.value_load(last_pair_i[0:1, :], min_val=15, max_val=63)
            select(0, 0)
            columns_read(0)
            pair(0, 0, 1, 0, True, False)
            with dve.Fori(1, final) as n:
                pair(n, n & 15, (n + 1) & 15, ((n + 1) >> 4) & 3, False, False)
            pair(final, 15, 0, 0, False, True)
            dve.wait_ge(scattered, final + 1)
            for b in range(4):
                h = x_sb[:, 2 * b:2 * b + 2, META:ALL]
                V.tensor_tensor(h, h, y_ps[:, 2 * b:2 * b + 2], ALU.add).then_inc(final_ready, 1)


def _chunk_columns():
    q, kv, rq, rv = HEADS * DH, 2 * DH, RH * RDK, RH * RDV
    base = {"q": 0, "k": q, "v": q + kv, "rq": q + 2 * kv}
    base["rk"] = base["rq"] + rq
    base["rv"] = base["rk"] + rq
    base["rg"] = base["rv"] + rv
    base["ga"] = base["rg"] + rv
    base["gr"] = base["ga"] + D
    a = np.arange(DH)

    def columns(kind, i):
        if kind == "q":
            return np.concatenate([i * DH + a, (i + PAIRS) * DH + a])
        return base[kind] + i * P + np.arange(P)
    return columns


def kernel(**inputs):
    import concourse.bacc as bacc
    from concourse.bass_utils import run_bass_kernel_spmd

    a = {k: np.asarray(v) for k, v in inputs.items()}
    h = np.concatenate([a["meta_tokens"], a["x"][0]], 0)
    xT = np.ascontiguousarray(h.T.reshape(KC, P, ALL).transpose(1, 0, 2))
    columns = _chunk_columns()
    w_in = a["w_in"][0]
    rows = np.concatenate([np.concatenate([j * DH + np.arange(DH), (j + PAIRS) * DH + np.arange(DH)])
                           for j in range(PAIRS)])
    full = {"wa": a["w_attn_branch"][0][rows], "wr": a["w_ret_branch"][0], "out": a["w_out"][0]}
    mix_w = np.empty((NU, P, KC, UCOL), np.float32)
    for c, (kind, i) in enumerate(CHUNKS):
        w = full[kind][:, i * P:(i + 1) * P] if kind in full else w_in[:, columns(kind, i)]
        mix_w[c // 2, :, :, (c % 2) * P:(c % 2 + 1) * P] = w.reshape(KC, P, P).transpose(1, 0, 2)
    mix_w = mix_w.reshape(NU, P, KC * UCOL)

    def by_feature(v):
        return v.reshape(KC, P).T

    params = np.concatenate([
        by_feature(a["mix_norm_gain"][0]), by_feature(a["ffn_norm_gain"][0]),
        np.tile(a["q_norm_gain"][0], 2)[:, None], np.tile(a["k_norm_gain"][0], 2)[:, None],
        np.broadcast_to(a["attn_sinks"][0].reshape(2, PAIRS).T.reshape(1, HEADS), (P, HEADS)),
        np.broadcast_to(a["b_router"], (P, EXPERTS)),
        a["w_router"][0].reshape(KC, P, EXPERTS).transpose(1, 0, 2).reshape(P, -1),
        a["b_gate_up"][0].reshape(EXPERTS, 16, P).transpose(2, 0, 1).reshape(P, -1)], 1)
    assert params.shape == (P, N_PARAM)
    arrays = {
        "xT": xT, "mix_w": mix_w, "consts": constants(), "params": np.ascontiguousarray(params),
        "b_down": np.ascontiguousarray(a["b_down"][0]), "w_gate_up": a["w_gate_up"][0], "w_down": a["w_down"][0],
    }
    nc = bacc.Bacc("TRN2", target_bir_lowering=False, num_devices=1)
    args = [nc.dram_tensor(f"in_{k}", v.shape, F32, kind="ExternalInput").ap() for k, v in arrays.items()]
    out = nc.dram_tensor("out", (P, KC, TOK), F32, kind="ExternalOutput").ap()
    build(nc, *args, out)
    r = run_bass_kernel_spmd(nc, [{f"in_{k}": v for k, v in arrays.items()}], core_ids=[0])
    y = np.asarray(r.results[0]["out"])
    return np.ascontiguousarray(y.transpose(2, 1, 0)).reshape(1, TOK, D)
```

```python
from contextlib import ExitStack

import numpy as np

import concourse.bass as bass
from concourse import mybir

F32 = mybir.dt.float32
I32 = mybir.dt.int32
U32 = mybir.dt.uint32
ALU = mybir.AluOpType
ACT = mybir.ActivationFunctionType
AX = mybir.AxisListType

P = 128
D = 1024
KC = D // P
META, TOK = 16, 256
ALL = META + TOK
BLK = 128
HEADS, DH = 16, 64
PAIRS = HEADS // 2
RH, RDK, RDV = 4, 128, 256
EXPERTS, TOPK, FF = 32, 4, 1024
EPS = 1e-5
ALPHA, LIMIT = 1.702, 7.0
SLOTS = 12
SPARES, REUSED = 6, 4
UCOL = 256
CAP = 64
B1K, B2K = META + BLK, META + 2 * BLK
SCW = B1K + B2K
MASKED = -1.0e30

UNITS = (["kv"] + ["q"] * 4 + ["rq"] * 2 + ["rk"] * 2 + ["rg"] * 4 + ["ga"] * 2 + ["rv"] * 4
         + ["wa"] * 2 + ["ga", "wa"] * 2 + ["gr", "wr"] * 4 + ["out"] * 4)
NU = len(UNITS)


def chunk_table():
    seen, table = {}, []
    for u in UNITS:
        for half in range(2):
            kind = ("k", "v")[half] if u == "kv" else u
            n = seen.get(kind, 0)
            table.append((kind, n))
            seen[kind] = n + 1
    return table


CHUNKS = chunk_table()
AT = {c: i for i, c in enumerate(CHUNKS)}

CONST_COLS = {}


def _const_layout():
    at = 0
    for name, n in (("ones", P), ("ident", P), ("heads2", P), ("halves", 2), ("eps", 1), ("eps64", 1), ("slopes", 2 * HEADS),
                    ("tri", P), ("iota", TOK), ("alibi", SCW), ("decay", RH * TOK), ("decay_meta", RH * TOK)):
        CONST_COLS[name] = (at, n)
        at += n
    return at


N_CONST = _const_layout()
N_CONST_EARLY = CONST_COLS["tri"][0]

PARAM_COLS = {}


def _param_layout():
    at = 0
    for name, n in (("mix_gain", KC), ("ffn_gain", KC), ("q_gain", 1), ("k_gain", 1), ("sinks", HEADS),
                    ("b_router", EXPERTS), ("w_router", KC * EXPERTS), ("b_gate_up", EXPERTS * 16)):
        PARAM_COLS[name] = (at, n)
        at += n
    return at


N_PARAM = _param_layout()


def constants():
    t = np.zeros((P, N_CONST), np.float64)

    def put(name, a):
        at, n = CONST_COLS[name]
        t[:a.shape[0], at:at + n] = a.reshape(a.shape[0], n)

    p = np.arange(P)
    put("ones", np.ones((P, P)))
    put("ident", np.eye(P))
    put("heads2", (p[:, None] // DH == p[None, :] // DH) * 1.0)
    put("halves", (p[:, None] // DH == np.arange(2)[None]) * 1.0)
    put("eps", np.full((P, 1), EPS))
    put("eps64", np.full((P, 1), DH * EPS))
    slope = 2.0 ** (-8.0 * np.arange(1, HEADS + 1) / HEADS)
    by_pair = np.stack([slope[:PAIRS], slope[PAIRS:]], 1)
    put("slopes", np.broadcast_to(by_pair[None, None], (P, 2, PAIRS, 2)))
    put("tri", (p[:, None] < p[None, :]) * 1.0)
    put("iota", np.broadcast_to(np.arange(TOK)[None], (P, TOK)))
    near = np.where(p[:, None] >= p[None, :], -(p[:, None] - p[None, :]), MASKED)
    far = np.where(p[None, :] > p[:, None], -(BLK + p[:, None] - p[None, :]), MASKED)
    m = np.arange(META)[None]
    put("alibi", np.concatenate([-(META + p[:, None] - m), near, -(META + BLK + p[:, None] - m), far, near], 1))
    gamma = 1.0 - 2.0 ** (-5.0 - np.arange(RH))
    q = np.arange(TOK)
    scale = RDK ** -0.5
    d1 = q[None, :] - p[:, None]
    put("decay", np.where(d1[:, None] >= 0, gamma[None, :, None] ** np.maximum(d1, 0)[:, None], 0.0) * scale)
    dm = META + q[None, :] - np.arange(META)[:, None]
    put("decay_meta", gamma[None, :, None] ** dm[:, None] * scale)
    return t.astype(np.float32)


def build(nc, xT, mix_w, consts, params, b_down, w_gate_up, w_down, out):
    with ExitStack() as ctx:
        def sem(name):
            return ctx.enter_context(nc.semaphore(name))

        ring = ctx.enter_context(nc.sbuf_tensor("ring", [P, SLOTS, 2048], F32))
        arena_bytes = 113280
        arena = ctx.enter_context(nc.sbuf_tensor("arena", [P, arena_bytes // 4], F32))
        cursor = [0]

        def region(cols):
            at = cursor[0]
            cursor[0] += cols
            assert cursor[0] * 4 <= arena_bytes, (cursor[0] * 4, arena_bytes)
            return arena[:, at:at + cols]

        def cut(reg, at, shape, parts=P):
            n = int(np.prod(shape))
            v = reg[0:parts, at:at + n]
            if len(shape) == 2:
                return v.rearrange("p (a b) -> p a b", b=shape[1])
            if len(shape) == 3:
                return v.rearrange("p (a b c) -> p a b c", b=shape[1], c=shape[2])
            return v

        x_sb = cut(region(KC * ALL), 0, (KC, ALL))
        r_u = region(KC * ALL)
        u_sb, u2T = cut(r_u, 0, (KC, ALL)), cut(r_u, 0, (KC, TOK))
        r_q = region(KC * TOK)
        qT, sig_rg, merged = (cut(r_q, 0, (KC, TOK)) for _ in range(3))
        u2tok = cut(r_q, 0, (2, D))
        r_att = region(KC * ALL)
        xsq, attT = cut(r_att, 0, (KC, ALL)), cut(r_att, 0, (PAIRS, TOK))
        e_gate, e_up = (cut(r_att, 1024 * i, (8, 2 * CAP)) for i in range(2))
        r_rg = region(KC * TOK)
        rgT = cut(r_rg, 0, (KC, TOK))
        e_sig, e_act = (cut(r_rg, 1024 * i, (8, 2 * CAP)) for i in range(2))
        r_gate = region(4 * TOK)
        gate_sb, e_out = cut(r_gate, 0, (4, TOK)), cut(r_gate, 0, (D,))
        r_rq = region(RH * TOK + RH * ALL)
        rqT, rkT = cut(r_rq, 0, (RH, TOK)), cut(r_rq, RH * TOK, (RH, ALL))
        xeT = cut(r_rq, 0, (KC, 2 * CAP))
        rt = 1024
        logits, chosen, wgt, posm = (cut(r_rq, rt + 64 * i, (2, EXPERTS)) for i in range(4))
        top8 = cut(r_rq, rt + 256, (2, 8))
        top8i = cut(r_rq, rt + 272, (2, 8)).bitcast(U32)
        top8f = cut(r_rq, rt + 288, (2, 8))
        neg_top, wsum, wrec = (cut(r_rq, rt + 304 + 2 * i, (2,)) for i in range(3))
        n_max, n_over, n_tmp = (cut(r_rq, rt + 310 + i, (1,)) for i in range(3))
        last_pair_i = cut(r_rq, rt + 314, (1,)).bitcast(I32)
        count = cut(r_rq, rt + 316, (EXPERTS,))
        root_tok, r_tok = (cut(r_rq, rt + 348 + 2 * i, (2,)) for i in range(2))
        wgtT = cut(r_rq, rt + 352, (TOK,), EXPERTS)
        r_rv = region(3 * D)
        kz = cut(r_rv, 0, (2, ALL))
        v_kv = cut(r_rv, 2 * ALL, (2, P))
        v_meta = cut(r_rv, 2 * ALL + 2 * P, (P,), META)
        rv_tok, rv_meta = cut(r_rv, 0, (2, D)), cut(r_rv, 2 * D, (D,), META)
        hsq = cut(r_rv, 0, (KC, TOK))
        gu_raw = cut(r_rv, 0, (16, P))
        r_p = region(2 * 2 * SCW + 4 * BLK + 6 * BLK)
        prob = cut(r_p, 0, (2, 2, SCW))
        probT_meta = cut(r_p, 4 * SCW, (4, BLK), META)
        probT = cut(r_p, 4 * SCW + 4 * BLK, (6, BLK))
        sel, selw, selwT = cut(r_p, 0, (2, 2 * CAP)), cut(r_p, 256, (2, 2 * CAP)), cut(r_p, 512, (TOK,))
        rs, rs_meta = cut(r_p, 0, (RH, 3 * BLK)), cut(r_p, RH * 3 * BLK, (RH, TOK), META)
        r_tmp = region(4 * 2 * TOK)
        tmp, sq = (cut(r_tmp, 1024 * i, (2, 2 * TOK)) for i in range(2))
        r_mix = region(ALL)
        root = region(ALL)
        par = region(N_PARAM)
        b_dn = cut(region(D), 0, (D,), EXPERTS)
        con = region(N_CONST)
        small = region(96)
        q_norm, q_rho, q_slope = (cut(small, 32 * i, (2, PAIRS, 2)) for i in range(3))
        v_tok = region(2)
        hit = r_gate[:, 0:2 * TOPK * EXPERTS].rearrange("p (t r e) -> p t r e", t=2, r=TOPK)
        soft = region(40)
        s_max, s_neg, s_sink, s_esink, s_sum, s_den, s_rec = (cut(soft, 4 * i, (2, 2)) for i in range(7))

        def const(name, parts=P):
            at, n = CONST_COLS[name]
            return con[0:parts, at:at + n]

        at = CONST_COLS["decay"][0]
        spare = (r_att[:, 0:2048], r_rg, r_tmp, con[:, at:at + 2048], r_p[:, 768:768 + 2048], r_u[:, 0:2048])
        assert len(spare) == SPARES

        def param(name):
            at, n = PARAM_COLS[name]
            return par[:, at:at + n]

        ones, ident = const("ones"), const("ident")
        decay = const("decay").rearrange("p (h q) -> p h q", h=RH)
        decay_meta = const("decay_meta", META).rearrange("p (h q) -> p h q", h=RH)
        sinks = param("sinks").rearrange("p (j x) -> p j x", x=2)
        w_rt = param("w_router").rearrange("p (k e) -> p k e", k=KC)
        b_gu = param("b_gate_up").rearrange("p (e c) -> p e c", e=EXPERTS)
        slopes = const("slopes").rearrange("p (b j x) -> p b j x", b=2, x=2)

        ps = ctx.enter_context(nc.psum_tensor("ps", [P, 8, 512], F32))
        PROJ, SCORE, PT_META, PT, PV = 0, 2, 4, 5, 7
        COUNT, WT, LOGIT = 2, 3, 3
        GATE, UP, Y = 0, 2, 4
        y_ps = ps[:, Y:Y + 4, :].rearrange("p b (c t) -> p (b c) t", t=TOK)

        landed = [sem(f"landed{i}") for i in range(SLOTS)]
        spare_landed = [sem(f"spare_landed{i}") for i in range(SPARES)]
        x_in = [sem("x_in0"), sem("x_in1")]
        early_in, params_in, late_in, bdown_in = sem("early_in"), sem("params_in"), sem("late_in"), sem("bdown_in")
        gained = sem("gained")
        squared = sem("squared")
        mix_stat = sem("mix_stat")
        mix_root = sem("mix_root")
        mix_r = sem("mix_r")
        zeros_set = sem("zeros_set")
        proj_done, proj_read = sem("proj_done"), sem("proj_read")
        k_sq, k_stat, k_root = sem("k_sq"), sem("k_stat"), sem("k_root")
        k_ready, v_turned, v_ready = sem("k_ready"), sem("v_turned"), sem("v_ready")
        q_sq, q_stat, q_root, q_ready = sem("q_sq"), sem("q_stat"), sem("q_root"), sem("q_ready")
        scored, score_read, biased = sem("scored"), sem("score_read"), sem("biased")
        exped, prob_ready = sem("exped"), sem("prob_ready")
        turned, turn_read, att_done, att_read = sem("turned"), sem("turn_read"), sem("att_done"), sem("att_read")
        sig_done = sem("sig_done")
        rv_turned, rv_read = sem("rv_turned"), sem("rv_read")
        rscored, rscore_read = sem("rscored"), sem("rscore_read")
        ret_done, ret_sq, ret_stat, ret_root, ret_ready = (sem("ret_done"), sem("ret_sq"), sem("ret_stat"),
                                                          sem("ret_root"), sem("ret_ready"))
        gate_sig = sem("gate_sig")
        h_sq, h_root, h_r, u2_ready = sem("h_sq"), sem("h_root"), sem("h_r"), sem("u2_ready")
        u2_turned, u2tok_ready = sem("u2_turned"), sem("u2tok_ready")
        logit_done, top_ready, route_exp = sem("logit_done"), sem("top_ready"), sem("route_exp")
        chosen_ready, counted, pairs_ready = sem("chosen_ready"), sem("counted"), sem("pairs_ready")
        wgt_ready, wgt_turned, wgtT_ready = sem("wgt_ready"), sem("wgt_turned"), sem("wgtT_ready")
        sel_ready, selw_ready = sem("sel_ready"), sem("selw_ready")
        units_used, first_half = sem("units_used"), sem("first_half")
        gathered, xe_ready = sem("gathered"), sem("xe_ready")
        raw_copied, gu_turned, gate_read = sem("raw_copied"), sem("gu_turned"), sem("gate_read")
        up_biased, gate_ready = sem("up_biased"), sem("gate_ready")
        sig_ready, act_ready, eout_ready = sem("sig_ready"), sem("act_ready"), sem("eout_ready")
        selw_turned, selwT_ready = sem("selw_turned"), sem("selwT_ready")
        summed, final_ready, stored = sem("summed"), sem("final_ready"), sem("stored")
        vec_step = sem("vec_step")

        def unit_place(n, q):
            pair_no = n if isinstance(n, int) else None
            if pair_no == 0 and SLOTS <= q < SLOTS + SPARES:
                return spare[q - SLOTS], spare_landed[q - SLOTS], 16
            if pair_no == 1 and 6 <= q < 6 + REUSED:
                i = SPARES - REUSED + q - 6
                return spare[i], spare_landed[i], 32
            if pair_no == 0 and q < SLOTS:
                skipped = 0
            elif pair_no == 0 or (pair_no == 1 and q < 6):
                skipped = SPARES
            else:
                skipped = SPARES + REUSED
            turn_no = NU + q - skipped
            return ring[:, turn_no % SLOTS], landed[turn_no % SLOTS], 32 * n + 16 * (turn_no // SLOTS + 1)

        block = ctx.enter_context(nc.Block())

        @block.sync
        def _(sp):
            for h in range(2):
                sp.dma_start(x_sb[:, 4 * h:4 * h + 4], xT[:, 4 * h:4 * h + 4]).then_inc(x_in[h], 16)
            for u in range(NU):
                if u >= SLOTS:
                    sp.wait_ge(proj_done, 2 * (u - SLOTS + 1))
                sp.dma_start(ring[:, u % SLOTS], mix_w[u]).then_inc(landed[u % SLOTS], 16)

            def pair_units(n, lap):
                pair_no = n if isinstance(n, int) else None
                for q in range(24):
                    j, x = divmod(q, 2)
                    if pair_no is None:
                        place, arrived, _ = unit_place(2, q)
                    else:
                        place, arrived, _ = unit_place(n, q)
                    if pair_no == 0 and q < SLOTS:
                        sp.wait_ge(proj_done, 2 * (NU + q - SLOTS + 1))
                    elif pair_no == 0 and q < SLOTS + SPARES:
                        if q == SLOTS + SPARES - 1:
                            sp.wait_ge(u2_turned, 2)
                    elif pair_no == 0 or (pair_no == 1 and q < 6):
                        sp.wait_ge(units_used, 24 * n + q - SLOTS - SPARES + 1)
                    elif pair_no == 1 and q < 6 + REUSED + SLOTS:
                        sp.wait_ge(units_used, 24 * n + q - SLOTS - REUSED + 1)
                    else:
                        sp.wait_ge(units_used, 24 * n + (q - SLOTS + 1))
                    e = bass.ds(2 * lap + x, 1)
                    if j < 8:
                        dst = place
                        src = w_gate_up[e, j * P:(j + 1) * P, :].rearrange("o p n -> (o p) n")
                    else:
                        r = 2 * (j - 8) * P
                        dst = place.rearrange("p (c n) -> p c n", c=2)
                        src = w_down[e, r:r + 2 * P, :].rearrange("o (c p) n -> (o p) c n", p=P)
                    sp.dma_start(dst, src).then_inc(arrived, 16)

            pair_units(0, 0)
            pair_units(1, 1)
            with sp.Fori(2, 15) as n:
                pair_units(n, n)
            sp.wait_ge(pairs_ready, 1)
            final = sp.value_load(last_pair_i[0:1, :], min_val=15, max_val=63)
            with sp.Fori(15, final + 1) as n:
                lap = sp.compute_val(n & 15)
                pair_units(n, lap)
            for b in range(4):
                sp.wait_ge(final_ready, b + 1)
                sp.dma_start(out[:, 2 * b:2 * b + 2], x_sb[:, 2 * b:2 * b + 2, META:ALL]).then_inc(stored, 16)
            sp.wait_ge(stored, 64)

        @block.gpsimd
        def _(pool):
            for n, v in enumerate((kz[DH:P, 0, :], kz[0:DH, 1, :])):
                if n >= 1:
                    pool.wait_ge(zeros_set, n)
                nc.gpsimd.memset(v, 0.0).then_inc(zeros_set, 1)

        @block.tensor
        def _(pe):
            mm, turn = nc.tensor.matmul, nc.tensor.transpose

            def project(c):
                kind, i = CHUNKS[c]
                unit, half = divmod(c, 2)
                if half == 0:
                    pe.wait_ge(landed[unit % SLOTS], 16 * (unit // SLOTS + 1))
                if c >= 2:
                    pe.wait_ge(proj_read, c - 1)
                if kind == "wa" and i == 0:
                    pe.wait_ge(att_read, PAIRS)
                if kind == "wr" and i == 0:
                    pe.wait_ge(ret_ready, RH)
                if kind == "out" and i == 0:
                    pe.wait_ge(proj_read, c)
                w = ring[:, unit % SLOTS].rearrange("p (k n) -> p k n", k=KC)
                for k in range(KC):
                    if kind == "wa":
                        rhs = attT[:, k]
                    elif kind == "wr":
                        rhs = rgT[:, k]
                    elif kind == "out":
                        rhs = merged[:, k]
                    elif kind in ("k", "v", "rk", "rv"):
                        rhs = u_sb[:, k]
                    else:
                        rhs = u_sb[:, k, META:ALL]
                    last = mm(ps[:, PROJ + half, 0:rhs.shape[-1]], w[:, k, half * P:(half + 1) * P], rhs,
                              start=(k == 0), stop=(k == KC - 1))
                last.then_inc(proj_done, 1)

            def mix_stats():
                for k in range(KC):
                    if k % 4 == 0:
                        pe.wait_ge(squared, k // 4 + 1)
                    last = mm(ps[:, SCORE, 0:ALL], ones, xsq[:, k], start=(k == 0), stop=(k == KC - 1))
                last.then_inc(mix_stat, 1)

            def mix_stats_by_token():
                for b in range(2):
                    for k in range(KC):
                        last = mm(ps[:, PV, 32 + b:33 + b], xsq[:, k, META + b * BLK:META + (b + 1) * BLK],
                                  ones[:, 0:1], start=(k == 0), stop=(k == KC - 1))
                last.then_inc(mix_stat, 1)

            def q_stats(j):
                pe.wait_ge(q_sq, j + 1)
                if j == 0:
                    pe.wait_ge(mix_root, 2)
                for b in range(2):
                    at = b * HEADS + 2 * j
                    last = mm(ps[:, PV, at:at + 2], sq[:, j % 2, b * BLK:(b + 1) * BLK], const("halves"),
                              start=True, stop=True)
                last.then_inc(q_stat, 1)

            def scores(j):
                if j == 0:
                    pe.wait_ge(q_ready, 1)
                    pe.wait_ge(k_ready, 2)
                    pe.wait_ge(zeros_set, 2)
                else:
                    pe.wait_ge(score_read, j)
                for x in range(2):
                    mm(ps[:, SCORE + x, 0:B1K], qT[:, j, 0:BLK], kz[:, x, 0:B1K], start=True, stop=True)
                    last = mm(ps[:, SCORE + x, B1K:SCW], qT[:, j, BLK:TOK], kz[:, x, :], start=True, stop=True)
                last.then_inc(scored, 1)

            def turn_probs(j):
                pe.wait_ge(prob_ready, j + 1)
                if j >= 1:
                    pe.wait_ge(turn_read, j)
                for x in range(2):
                    p_x = prob[:, j % 2, x]
                    for b, at in ((0, 0), (1, B1K)):
                        turn(ps[0:META, PT_META, (2 * b + x) * BLK:(2 * b + x + 1) * BLK], p_x[:, at:at + META], ident)
                    for c, at in enumerate((META, B1K + META, B1K + META + BLK)):
                        last = turn(ps[:, PT + x, c * BLK:(c + 1) * BLK], p_x[:, at:at + BLK], ident)
                last.then_inc(turned, 1)

            def attend(j):
                if j == 0:
                    pe.wait_ge(v_ready, 1)
                    pe.wait_ge(q_root, 2)
                else:
                    pe.wait_ge(att_read, j)
                pe.wait_ge(turn_read, j + 1)
                for b in range(2):
                    for c in range(-1, b + 1):
                        for x in range(2):
                            f = slice(x * DH, (x + 1) * DH)
                            o = ps[f, PV, b * BLK:(b + 1) * BLK]
                            if c < 0:
                                mm(o, v_meta[:, f], probT_meta[:, 2 * b + x], start=True, stop=False)
                            else:
                                last = mm(o, v_kv[:, c, f], probT[:, 3 * x + b + c], start=False, stop=(c == b))
                last.then_inc(att_done, 1)

            def turn_value(i):
                bank = PT_META + i % 2
                pe.wait_ge(proj_read, AT[("rv", i)] + 1)
                if i >= 2:
                    pe.wait_ge(rv_read, i - 1)
                t = tmp[:, i % 2]
                turn(ps[0:META, bank, 0:P], t[:, 0:META], ident)
                turn(ps[:, bank, P:2 * P], t[:, META:META + BLK], ident)
                turn(ps[:, bank, 2 * P:3 * P], t[:, META + BLK:ALL], ident).then_inc(rv_turned, 1)

            def ret_scores(h):
                if h == 0:
                    pe.wait_ge(score_read, PAIRS)
                else:
                    pe.wait_ge(rscore_read, h)
                q = rqT[:, h]
                mm(ps[:, SCORE, 0:TOK], rkT[:, h, META:META + BLK], q, start=True, stop=True)
                mm(ps[:, SCORE, TOK:TOK + BLK], rkT[:, h, META + BLK:ALL], q[:, BLK:TOK], start=True, stop=True)
                mm(ps[0:META, SCORE + 1, 0:TOK], rkT[:, h, 0:META], q, start=True, stop=True).then_inc(rscored, 1)

            def ret_bank(h):
                return (SCORE, SCORE + 1, PT + 1, PV)[h]

            def retain(h):
                pe.wait_ge(rscore_read, RH)
                pe.wait_ge(rv_read, 2 * RH)
                bank = ret_bank(h)
                for v in range(2):
                    f = slice((2 * h + v) * P, (2 * h + v + 1) * P)
                    o = ps[:, bank, v * TOK:(v + 1) * TOK]
                    mm(o, rv_meta[:, f], rs_meta[:, h], start=True, stop=False, skip_group_check=True)
                    mm(o, rv_tok[:, 0, f], rs[:, h, 0:TOK], start=False, stop=False, skip_group_check=True)
                    last = mm(o[:, BLK:TOK], rv_tok[:, 1, f], rs[:, h, TOK:TOK + BLK], start=False, stop=True,
                              skip_group_check=True)
                last.then_inc(ret_done, 1)

            def ret_stats(h):
                pe.wait_ge(ret_sq, h + 1)
                bank = PT_META + h % 2
                if h >= 2:
                    pe.wait_ge(ret_root, h - 1)
                for v in range(2):
                    last = mm(ps[:, bank, 0:TOK], ones, sq[:, h % 2, v * TOK:(v + 1) * TOK], start=(v == 0), stop=(v == 1))
                last.then_inc(ret_stat, 1)

            pe.wait_ge(early_in, 16)
            mix_stats()
            pe.wait_ge(gained, 2)
            project(0)
            project(1)
            mix_stats_by_token()
            project(2)
            pe.wait_ge(k_sq, 1)
            mm(ps[:, PT + 1, 0:ALL], const("heads2"), sq[:, 0, 0:ALL], start=True, stop=True).then_inc(k_stat, 1)
            pe.wait_ge(proj_read, AT[("v", 0)] + 1)
            turn(ps[0:META, PT_META, 0:P], tmp[:, 1, 0:META], ident)
            turn(ps[:, PT, 0:P], tmp[:, 1, META:META + BLK], ident)
            turn(ps[:, PT, P:2 * P], tmp[:, 1, META + BLK:ALL], ident).then_inc(v_turned, 1)
            for j in range(PAIRS):
                project(AT[("q", j)] + 1)
                q_stats(j)
            for i in range(PAIRS + 1):
                c = AT[("rq", 0)] + 2 * i
                if i > 0:
                    project(c)
                    turn_probs(i - 1)
                if i < PAIRS:
                    scores(i)
                project(c + 1)
                if i > 0:
                    attend(i - 1)
            project(AT[("ga", 2)])
            project(AT[("ga", 3)])
            for h in range(RH):
                project(AT[("rv", 2 * h)])
                if h > 0:
                    turn_value(2 * h - 1)
                ret_scores(h)
                project(AT[("rv", 2 * h + 1)])
                turn_value(2 * h)
            project(AT[("wa", 0)])
            turn_value(2 * RH - 1)
            project(AT[("wa", 1)])
            retain(0)
            retain(1)
            project(AT[("wa", 2)])
            ret_stats(0)
            retain(2)
            project(AT[("wa", 3)])
            ret_stats(1)
            retain(3)
            project(AT[("ga", 4)])
            ret_stats(2)
            project(AT[("ga", 5)])
            ret_stats(3)
            for c in range(AT[("ga", 5)] + 1, AT[("out", 0)]):
                project(c)

            def route(k):
                pe.wait_ge(u2_ready, k + 1)
                pe.wait_ge(h_sq, k + 1)
                for t in range(2):
                    block_t = slice(t * P, (t + 1) * P)
                    mm(ps[:, LOGIT, t * EXPERTS:(t + 1) * EXPERTS], u2T[:, k, block_t], w_rt[:, k],
                       start=(k == 0 and t == 0), stop=(k == KC - 1), skip_group_check=True)
                    at = 2 * EXPERTS + t
                    last = mm(ps[:, LOGIT, at:at + 1], hsq[:, k, block_t], ones[:, 0:1],
                              start=False, stop=(k == KC - 1), skip_group_check=True)
                last.then_inc(logit_done, 1)

            for k in range(KC):
                project(AT[("out", k)])
                if k >= 1:
                    route(k - 1)
            route(KC - 1)
            for t in range(2):
                for k in range(KC):
                    last = turn(ps[:, Y + 2 * t + k // 4, (k % 4) * P:(k % 4 + 1) * P], u2T[:, k, t * P:(t + 1) * P], ident)
                last.then_inc(u2_turned, 1)
            pe.wait_ge(chosen_ready, 1)
            mm(ps[:, COUNT, 0:EXPERTS], const("tri"), chosen[:, 0], start=True, stop=True)
            mm(ps[:, COUNT, EXPERTS:2 * EXPERTS], ones, chosen[:, 0], start=True, stop=False)
            mm(ps[:, COUNT, EXPERTS:2 * EXPERTS], const("tri"), chosen[:, 1], start=False, stop=True)
            mm(ps[:, COUNT, 2 * EXPERTS:3 * EXPERTS], ones, chosen[:, 0], start=True, stop=False)
            mm(ps[:, COUNT, 2 * EXPERTS:3 * EXPERTS], ones, chosen[:, 1], start=False, stop=True).then_inc(counted, 1)

            def gather():
                for k in range(KC):
                    o = ps[:, GATE + k // 4, (k % 4) * P:(k % 4 + 1) * P]
                    for t in range(2):
                        last = mm(o, u2tok[:, t, k * P:(k + 1) * P], sel[:, t], start=(t == 0), stop=(t == 1))
                last.then_inc(gathered, 1)

            def unit_landed(n, q):
                place, arrived, value = unit_place(n, q)
                pe.wait_ge(arrived, value)
                return place

            def gate_up(n):
                pe.wait_ge(xe_ready, n + 1)
                if not (isinstance(n, int) and n == 0):
                    pe.wait_ge(eout_ready, 2 * n)
                    pe.wait_ge(selwT_ready, n)
                for q in range(16):
                    j, x = divmod(q, 2)
                    w, half = unit_landed(n, q), slice(x * CAP, (x + 1) * CAP)
                    for b in range(4):
                        last = mm(ps[half, GATE + b], xeT[:, j, half], w[:, b * 512:(b + 1) * 512],
                                  start=(j == 0), stop=(j == 7))
                    last.then_inc(units_used, 1)

            def turn_hidden(n):
                pe.wait_ge(raw_copied, 2 * n + 2)
                for c in range(16):
                    last = turn(ps[:, GATE + c // 4, (c % 4) * P:(c % 4 + 1) * P], gu_raw[:, c], ident)
                last.then_inc(gu_turned, 1)

            def turn_weighted(n, last_pair):
                pe.wait_ge(selw_ready, n + 1)
                if last_pair:
                    pe.wait_ge(gate_read, n + 1)
                else:
                    pe.wait_ge(xe_ready, n + 2)
                for t in range(2):
                    last = turn(ps[:, GATE, t * P:(t + 1) * P], selw[:, t], ident)
                last.then_inc(selw_turned, 1)

            def down(n, last_pair):
                pe.wait_ge(act_ready, n + 1)
                for q in range(16, 24):
                    if q == 22:
                        turn_weighted(n, last_pair)
                    j, x = divmod(q, 2)
                    w, half = unit_landed(n, q), slice(x * CAP, (x + 1) * CAP)
                    for b in range(2):
                        for f in range(2):
                            k = 2 * (j - 8) + f
                            last = mm(ps[half, UP + b], e_act[:, k, half],
                                      w[:, f * D + b * 512:f * D + (b + 1) * 512], start=(k == 0), stop=(k == 7))
                        if q == 23 and b == 0:
                            last.then_inc(first_half, 1)
                    last.then_inc(units_used, 1)

            def add_back(c0, c1):
                for c in range(c0, c1):
                    last = mm(y_ps[:, c], e_out[:, c * P:(c + 1) * P], selwT, start=False, stop=False,
                              skip_group_check=True)
                return last

            def start_output(c0, c1):
                pe.wait_ge(bdown_in, 16)
                for c in range(c0, c1):
                    mm(y_ps[:, c], b_dn[:, c * P:(c + 1) * P], wgtT, start=(c % 2 == 0), stop=False,
                       skip_group_check=True)

            def pair(n, first, last_pair):
                gate_up(n)
                if first:
                    start_output(4, KC)
                else:
                    add_back(0, 4)
                turn_hidden(n)
                if not first:
                    add_back(4, KC)
                if not last_pair:
                    pe.wait_ge(sel_ready, n + 2)
                    pe.wait_ge(gate_read, n + 1)
                    gather()
                down(n, last_pair)

            pe.wait_ge(wgt_ready, 1)
            for t in range(2):
                last = turn(ps[0:EXPERTS, WT, t * P:(t + 1) * P], wgt[:, t], ident)
            last.then_inc(wgt_turned, 1)
            pe.wait_ge(u2tok_ready, 2)
            pe.wait_ge(sel_ready, 1)
            gather()
            pe.wait_ge(wgtT_ready, 1)
            start_output(0, 4)
            pair(0, True, False)
            pe.wait_ge(pairs_ready, 1)
            final = pe.value_load(last_pair_i[0:1, :], min_val=15, max_val=63)
            pair(1, False, False)
            with pe.Fori(2, final) as n:
                pair(n, False, False)
            pair(final, False, True)
            pe.wait_ge(selwT_ready, final + 1)
            for b in range(4):
                pe.wait_ge(eout_ready, 2 * final + 1 + b // 2)
                add_back(2 * b, 2 * b + 2).then_inc(summed, 1)

        @block.scalar
        def _(act):
            A = nc.scalar.activation
            act.dma_start(con[:, 0:N_CONST_EARLY], consts[:, 0:N_CONST_EARLY]).then_inc(early_in, 16)
            act.dma_start(par, params).then_inc(params_in, 16)
            act.dma_start(con[:, N_CONST_EARLY:N_CONST], consts[:, N_CONST_EARLY:N_CONST]).then_inc(late_in, 16)
            act.dma_start(b_dn, b_down).then_inc(bdown_in, 16)
            for h in range(2):
                act.wait_ge(x_in[h], 16)
                A(xsq[:, 4 * h:4 * h + 4], x_sb[:, 4 * h:4 * h + 4], ACT.Square).then_inc(squared, 1)
            act.wait_ge(early_in, 16)
            act.wait_ge(mix_stat, 1)
            A(root, ps[:, SCORE, 0:ALL], ACT.Sqrt, bias=const("eps"), scale=1.0 / D).then_inc(mix_root, 1)
            act.wait_ge(params_in, 16)
            act.wait_ge(proj_read, 1)
            A(sq[:, 0, 0:ALL], tmp[:, 0, 0:ALL], ACT.Square).then_inc(k_sq, 1)

            def query(j):
                c = AT[("q", j)]
                act.wait_ge(proj_done, c + 1)
                if j >= 2:
                    act.wait_ge(q_stat, j - 1)
                if j == 0:
                    act.wait_ge(k_stat, 1)
                A(sq[:, j % 2, 0:TOK], ps[:, PROJ + c % 2, 0:TOK], ACT.Square).then_inc(q_sq, 1)
                act.wait_ge(proj_read, c)
                A(qT[:, j], ps[:, PROJ + c % 2, 0:TOK], ACT.Copy, scale=param("q_gain")).then_inc(proj_read, 1)

            act.wait_ge(mix_stat, 2)
            A(v_tok, ps[:, PV, 32:34], ACT.Copy, scale=1.0 / D).then_inc(mix_root, 1)
            query(0)
            act.wait_ge(mix_r, 1)
            A(root, ps[:, PT + 1, 0:ALL], ACT.Sqrt, bias=const("eps"), scale=1.0 / DH).then_inc(k_root, 1)
            act.wait_ge(v_turned, 1)
            A(v_meta, ps[0:META, PT_META, 0:P], ACT.Copy)
            A(v_kv, ps[:, PT, 0:2 * P].rearrange("p (c f) -> p c f", c=2), ACT.Copy).then_inc(v_ready, 1)
            for j in range(1, PAIRS):
                query(j)
            act.wait_ge(q_stat, PAIRS)
            act.wait_ge(mix_r, 2)
            for b in range(2):
                A(q_norm[:, b], ps[:, PV, b * HEADS:(b + 1) * HEADS].rearrange("p (j x) -> p j x", x=2), ACT.Sqrt,
                  bias=v_tok[:, b:b + 1]).then_inc(q_root, 1)

            for i in range(PAIRS + 1):
                if i > 0:
                    j = i - 1
                    act.wait_ge(turned, j + 1)
                    if j >= 1:
                        act.wait_ge(att_done, j)
                    A(probT_meta, ps[0:META, PT_META].rearrange("p (a b) -> p a b", b=BLK), ACT.Copy)
                    A(probT.rearrange("p (x c) q -> p x (c q)", x=2), ps[:, PT:PT + 2, 0:3 * BLK],
                      ACT.Copy).then_inc(turn_read, 1)
                if i < PAIRS:
                    act.wait_ge(biased, i + 1)
                    for x in range(2):
                        for b, (lo, hi) in enumerate(((0, B1K), (B1K, SCW))):
                            v = prob[:, i % 2, x, lo:hi]
                            A(v, v, ACT.Exp, bias=s_neg[:, b, x:x + 1], scale=q_rho[:, b, i, x:x + 1],
                              accum_out=s_sum[:, b, x:x + 1])
                    A(s_esink, s_sink, ACT.Exp).then_inc(exped, 1)
                if i > 0:
                    act.wait_ge(att_done, i)
                    A(attT[:, i - 1], ps[:, PV, 0:TOK], ACT.Copy).then_inc(att_read, 1)

            act.wait_ge(proj_read, AT[("ga", 3)] + 1)
            for h in range(RH):
                A(sig_rg[:, 2 * h:2 * h + 2], rgT[:, 2 * h:2 * h + 2], ACT.Sigmoid).then_inc(sig_done, 1)
            A(gate_sb, gate_sb, ACT.Sigmoid).then_inc(gate_sig, 4)

            def value_read(i):
                act.wait_ge(rv_turned, i + 1)
                bank = PT_META + i % 2
                f = slice(i * P, (i + 1) * P)
                A(rv_meta[:, f], ps[0:META, bank, 0:P], ACT.Copy)
                A(rv_tok[:, :, f], ps[:, bank, P:3 * P].rearrange("p (c f) -> p c f", c=2), ACT.Copy).then_inc(rv_read, 1)

            for i in range(2 * RH):
                value_read(i)

            def ret_bank(h):
                return (SCORE, SCORE + 1, PT + 1, PV)[h]

            def ret_square(h):
                act.wait_ge(ret_done, h + 1)
                if h >= 2:
                    act.wait_ge(ret_stat, h - 1)
                A(sq[:, h % 2], ps[:, ret_bank(h)], ACT.Square).then_inc(ret_sq, 1)

            def ret_sqrt(h):
                act.wait_ge(ret_stat, h + 1)
                if h >= 1:
                    act.wait_ge(ret_ready, h)
                A(root[:, 0:TOK], ps[:, PT_META + h % 2, 0:TOK], ACT.Sqrt, bias=const("eps"),
                  scale=1.0 / RDV).then_inc(ret_root, 1)

            ret_square(0)
            ret_square(1)
            ret_sqrt(0)
            ret_square(2)
            ret_sqrt(1)
            ret_square(3)
            ret_sqrt(2)
            ret_sqrt(3)
            for kind in ("ga", "gr"):
                for i in range(4 if kind == "ga" else 0, KC):
                    act.wait_ge(proj_read, AT[(kind, i)] + 1)
                    A(gate_sb[:, i % 4], gate_sb[:, i % 4], ACT.Sigmoid).then_inc(gate_sig, 1)
            for k in range(KC):
                act.wait_ge(proj_read, AT[("out", k)] + 1)
                A(hsq[:, k], x_sb[:, k, META:ALL], ACT.Square).then_inc(h_sq, 1)
            act.wait_ge(logit_done, KC)
            A(root_tok, ps[:, LOGIT, 2 * EXPERTS:2 * EXPERTS + 2], ACT.Sqrt, bias=const("eps"),
              scale=1.0 / D).then_inc(h_root, 1)
            act.wait_ge(top_ready, 1)
            for t in range(2):
                A(wgt[:, t], logits[:, t], ACT.Exp, bias=neg_top[:, t:t + 1]).then_inc(route_exp, 1)
            act.wait_ge(h_r, 1)
            for t in range(2):
                act.wait_ge(u2_turned, t + 1)
                A(u2tok[:, t].rearrange("p (b f) -> p b f", b=2), ps[:, Y + 2 * t:Y + 2 * t + 2], ACT.Copy,
                  scale=r_tok[:, t:t + 1]).then_inc(u2tok_ready, 1)
            act.wait_ge(wgt_turned, 1)
            A(wgtT, ps[0:EXPERTS, WT, 0:TOK], ACT.Copy).then_inc(wgtT_ready, 1)

            def pair(n):
                act.wait_ge(units_used, 24 * n + 16)
                A(gu_raw[:, 0:8].rearrange("p (b c) f -> p b (c f)", b=2), ps[:, GATE:GATE + 2],
                  ACT.Copy).then_inc(raw_copied, 1)
                act.wait_ge(gate_ready, n + 1)
                A(e_sig, e_gate, ACT.Sigmoid, scale=ALPHA).then_inc(sig_ready, 1)
                act.wait_ge(selw_turned, n + 1)
                A(selwT, ps[:, GATE, 0:TOK], ACT.Copy).then_inc(selwT_ready, 1)
                act.wait_ge(first_half, n + 1)
                A(e_out[:, 0:512], ps[:, UP], ACT.Copy).then_inc(eout_ready, 1)
                act.wait_ge(units_used, 24 * n + 24)
                A(e_out[:, 512:D], ps[:, UP + 1], ACT.Copy).then_inc(eout_ready, 1)

            act.wait_ge(pairs_ready, 1)
            final = act.value_load(last_pair_i[0:1, :], min_val=15, max_val=63)
            with act.Fori(0, final + 1) as n:
                pair(n)

        @block.vector
        def _(dve):
            V = nc.vector
            steps = [0]

            def link(ins):
                steps[0] += 1
                ins.then_inc(vec_step, 1)
                dve.wait_ge(vec_step, steps[0])

            dve.wait_ge(params_in, 16)
            for h in range(2):
                dve.wait_ge(x_in[h], 16)
                for k in range(4 * h, 4 * h + 4):
                    last = V.tensor_scalar(u_sb[:, k], x_sb[:, k], param("mix_gain")[:, k:k + 1], None, ALU.mult)
                last.then_inc(gained, 1)
            dve.wait_ge(mix_root, 1)
            V.reciprocal(r_mix, root).then_inc(mix_r, 1)
            dve.wait_ge(mix_r, 1)

            def evict(c, dst):
                n = dst.shape[-1]
                dve.wait_ge(proj_done, c + 1)
                V.tensor_tensor(dst, ps[:, PROJ + c % 2, 0:n], r_mix[:, ALL - n:ALL], ALU.mult).then_inc(proj_read, 1)

            evict(0, tmp[:, 0, 0:ALL])
            evict(1, tmp[:, 1, 0:ALL])
            dve.wait_ge(k_root, 1)
            dve.wait_ge(proj_read, 2)
            link(V.reciprocal(root, root))
            dve.wait_ge(zeros_set, 2)
            for x in range(2):
                f = slice(x * DH, (x + 1) * DH)
                V.scalar_tensor_tensor(kz[f, x], tmp[f, 0, 0:ALL], param("k_gain")[f], root[f], ALU.mult,
                                       ALU.mult).then_inc(k_ready, 1)
            dve.wait_ge(mix_root, 2)
            V.tensor_scalar(v_tok, v_tok, EPS, DH * EPS, ALU.add, ALU.mult).then_inc(mix_r, 1)
            dve.wait_ge(q_root, 2)
            V.reciprocal(q_rho, q_norm).then_inc(q_ready, 1)
            dve.wait_ge(late_in, 16)
            link(V.tensor_tensor(q_slope, q_norm, slopes, ALU.mult))

            def place_of(c):
                kind, i = CHUNKS[c]
                return {"rq": rqT, "rk": rkT, "rg": rgT, "ga": gate_sb}[kind][:, i]

            def bias_scores(i):
                dve.wait_ge(scored, i + 1)
                for x in range(2):
                    for b, (lo, hi) in enumerate(((0, B1K), (B1K, SCW))):
                        last = V.scalar_tensor_tensor(prob[:, i % 2, x, lo:hi], const("alibi")[:, lo:hi],
                                                      q_slope[:, b, i, x:x + 1], ps[:, SCORE + x, lo:hi],
                                                      ALU.mult, ALU.add)
                last.then_inc(score_read, 1)
                dve.wait_ge(score_read, i + 1)
                V.tensor_reduce(s_max[:, 0], prob[:, i % 2, :, 0:B1K], AX.X, ALU.max)
                link(V.tensor_reduce(s_max[:, 1], prob[:, i % 2, :, B1K:SCW], AX.X, ALU.max))
                link(V.tensor_tensor(s_max, s_max, q_rho[:, :, i], ALU.mult))
                sink = sinks[:, i:i + 1].to_broadcast([P, 2, 2])
                link(V.tensor_tensor(s_max, s_max, sink, ALU.max))
                if i >= 1:
                    dve.wait_ge(exped, i)
                V.tensor_scalar(s_neg, s_max, -1.0, None, ALU.mult)
                V.tensor_tensor(s_sink, sink, s_max, ALU.subtract).then_inc(biased, 1)

            def normalise(i):
                dve.wait_ge(exped, i + 1)
                link(V.tensor_tensor(s_den, s_sum, s_esink, ALU.add))
                link(V.reciprocal(s_rec, s_den))
                for x in range(2):
                    for b, (lo, hi) in enumerate(((0, B1K), (B1K, SCW))):
                        v = prob[:, i % 2, x, lo:hi]
                        last = V.tensor_scalar(v, v, s_rec[:, b, x:x + 1], None, ALU.mult)
                last.then_inc(prob_ready, 1)

            evict_first = AT[("rq", 0)]
            dve.wait_ge(proj_read, evict_first)
            for i in range(PAIRS + 1):
                c = AT[("rq", 0)] + 2 * i
                evict(c, place_of(c))
                if i < PAIRS:
                    bias_scores(i)
                evict(c + 1, place_of(c + 1))
                if i < PAIRS:
                    normalise(i)
            evict(AT[("ga", 2)], gate_sb[:, 2])
            evict(AT[("ga", 3)], gate_sb[:, 3])
            for h in range(RH):
                for v in range(2):
                    i = 2 * h + v
                    if i >= 2:
                        dve.wait_ge(rv_turned, i - 1)
                    if i == 0:
                        dve.wait_ge(att_done, PAIRS)
                    evict(AT[("rv", i)], tmp[:, i % 2, 0:ALL])
                    if v == 0:
                        dve.wait_ge(rscored, h + 1)
                        V.tensor_tensor(rs[:, h, 0:TOK], ps[:, SCORE, 0:TOK], decay[:, h], ALU.mult)
                        V.tensor_tensor(rs[:, h, TOK:TOK + BLK], ps[:, SCORE, TOK:TOK + BLK], decay[:, h, 0:BLK], ALU.mult)
                        V.tensor_tensor(rs_meta[:, h], ps[0:META, SCORE + 1, 0:TOK], decay_meta[:, h],
                                        ALU.mult).then_inc(rscore_read, 1)
                dve.wait_ge(sig_done, h + 1)
                link(V.tensor_tensor(rgT[:, 2 * h:2 * h + 2], rgT[:, 2 * h:2 * h + 2], sig_rg[:, 2 * h:2 * h + 2], ALU.mult))

            def ret_out(h):
                bank = (SCORE, SCORE + 1, PT + 1, PV)[h]
                dve.wait_ge(ret_root, h + 1)
                rr = tmp[:, 0, 0:TOK]
                link(V.reciprocal(rr, root[:, 0:TOK]))
                g = rgT[:, 2 * h:2 * h + 2]
                link(V.tensor_tensor(g, g, rr.rearrange("p (o t) -> p o t", o=1).to_broadcast([P, 2, TOK]), ALU.mult))
                V.tensor_tensor(g, g, ps[:, bank].rearrange("p (v t) -> p v t", v=2), ALU.mult).then_inc(ret_ready, 1)

            def merge(c):
                kind, i = CHUNKS[c]
                b = ps[:, PROJ + c % 2, 0:TOK]
                if kind in ("ga", "gr"):
                    if i >= 4 or kind == "gr":
                        evict(c, gate_sb[:, i % 4])
                elif kind == "wa":
                    dve.wait_ge(gate_sig, i + 1)
                    dve.wait_ge(proj_done, c + 1)
                    V.tensor_tensor(merged[:, i], b, gate_sb[:, i % 4], ALU.mult).then_inc(proj_read, 1)
                elif kind == "wr":
                    dve.wait_ge(gate_sig, KC + i + 1)
                    dve.wait_ge(proj_done, c + 1)
                    gated = tmp[:, (i + 1) % 2, 0:TOK]
                    link(V.tensor_tensor(gated, b, gate_sb[:, i % 4], ALU.mult))
                    V.tensor_tensor(merged[:, i], merged[:, i], gated, ALU.add).then_inc(proj_read, 1)
                elif kind == "out":
                    dve.wait_ge(proj_done, c + 1)
                    h = x_sb[:, i, META:ALL]
                    V.tensor_tensor(h, h, b, ALU.add).then_inc(proj_read, 1)
                    dve.wait_ge(proj_read, c + 1)
                    V.tensor_scalar(u2T[:, i], h, param("ffn_gain")[:, i:i + 1], None, ALU.mult).then_inc(u2_ready, 1)

            for c in range(AT[("wa", 0)], len(CHUNKS)):
                merge(c)
                if c == AT[("wa", 3)]:
                    ret_out(0)
                if c == AT[("ga", 4)]:
                    ret_out(1)
                if c == AT[("ga", 5)]:
                    ret_out(2)
                if c == AT[("ga", 5)] + 1:
                    ret_out(3)

            dve.wait_ge(h_root, 1)
            V.reciprocal(r_tok, root_tok).then_inc(h_r, 1)
            dve.wait_ge(h_r, 1)
            for t in range(2):
                last = V.scalar_tensor_tensor(logits[:, t], ps[:, LOGIT, t * EXPERTS:(t + 1) * EXPERTS], r_tok[:, t:t + 1],
                                              param("b_router"), ALU.mult, ALU.add)
            link(last)
            for t in range(2):
                last = V.max(top8[:, t], logits[:, t])
            link(last)
            V.tensor_scalar(neg_top, top8[:, :, 0], -1.0, None, ALU.mult).then_inc(top_ready, 1)
            for t in range(2):
                last = V.max_index(top8i[:, t], top8[:, t], logits[:, t])
            link(last)
            link(V.tensor_copy(top8f, top8i))
            i32 = const("iota")[:, 0:EXPERTS].rearrange("p (a b e) -> p a b e", a=1, b=1)
            link(V.tensor_tensor(hit, i32.to_broadcast([P, 2, TOPK, EXPERTS]),
                                 top8f[:, :, 0:TOPK].rearrange("p t (r o) -> p t r o", o=1).to_broadcast(
                                     [P, 2, TOPK, EXPERTS]), ALU.is_equal))
            link(V.tensor_tensor(hit[:, :, 0:2], hit[:, :, 0:2], hit[:, :, 2:4], ALU.add))
            V.tensor_tensor(chosen, hit[:, :, 0], hit[:, :, 1], ALU.add).then_inc(chosen_ready, 1)
            dve.wait_ge(chosen_ready, 1)
            dve.wait_ge(route_exp, 2)
            link(V.tensor_tensor(wgt, wgt, chosen, ALU.mult))
            link(V.tensor_reduce(wsum, wgt, AX.X, ALU.add))
            dve.wait_ge(counted, 1)
            pos = ps[:, COUNT, 0:2 * EXPERTS].rearrange("p (t e) -> p t e", t=2)
            link(V.scalar_tensor_tensor(posm, pos, 1.0, chosen, ALU.add, ALU.mult))
            V.tensor_copy(count, ps[:, COUNT, 2 * EXPERTS:3 * EXPERTS])
            link(V.tensor_scalar(posm, posm, -1.0, None, ALU.add))

            def select(lap, rnd):
                place = posm[:, :, bass.ds(2 * lap, 2)]
                col = const("iota")[:, bass.ds(CAP * rnd, CAP)]
                V.tensor_tensor(sel.rearrange("p t (x s) -> p t x s", x=2),
                                col.rearrange("p (a b s) -> p a b s", a=1, b=1).to_broadcast([P, 2, 2, CAP]),
                                place.rearrange("p t (x o) -> p t x o", o=1).to_broadcast([P, 2, 2, CAP]),
                                ALU.is_equal).then_inc(sel_ready, 1)

            def weigh(n, lap):
                w = wgt[:, :, bass.ds(2 * lap, 2)]
                dve.wait_ge(sel_ready, n + 1)
                V.tensor_tensor(selw.rearrange("p t (x s) -> p t x s", x=2), sel.rearrange("p t (x s) -> p t x s", x=2),
                                w.rearrange("p t (x o) -> p t x o", o=1).to_broadcast([P, 2, 2, CAP]),
                                ALU.mult).then_inc(selw_ready, 1)

            def columns_read(n):
                dve.wait_ge(gathered, n + 1)
                V.tensor_copy(xeT.rearrange("p (b c) s -> p b (c s)", b=2), ps[:, GATE:GATE + 2]).then_inc(xe_ready, 1)

            def hidden(n, lap):
                def link(ins, k):
                    ins.then_inc(vec_step, 1)
                    dve.wait_ge(vec_step, 2 * n + step0 + k)

                def biased(out, bank, half, sem_read, sem_value):
                    for b in range(2):
                        at = 8 * half + 4 * b
                        bias = b_gu[:, bass.ds(2 * lap, 2), at:at + 4].rearrange("p x (k s) -> p k x s", s=1)
                        last = V.tensor_tensor(out[:, 4 * b:4 * b + 4].rearrange("p k (x s) -> p k x s", x=2),
                                               ps[:, bank + b].rearrange("p (k x s) -> p k x s", k=4, x=2),
                                               bias.to_broadcast([P, 4, 2, CAP]), ALU.add)
                    last.then_inc(sem_read, 1)
                    dve.wait_ge(sem_read, sem_value)

                dve.wait_ge(units_used, 24 * n + 16)
                V.tensor_copy(gu_raw[:, 8:16].rearrange("p (b c) f -> p b (c f)", b=2),
                              ps[:, UP:UP + 2]).then_inc(raw_copied, 1)
                dve.wait_ge(gu_turned, n + 1)
                biased(e_gate, GATE, 0, gate_read, n + 1)
                V.tensor_scalar(e_gate, e_gate, LIMIT, None, ALU.min).then_inc(gate_ready, 1)
                biased(e_up, UP, 1, up_biased, n + 1)
                link(V.tensor_scalar(e_up, e_up, LIMIT, -LIMIT, ALU.min, ALU.max), 1)
                link(V.scalar_tensor_tensor(e_up, e_up, 1.0, e_gate, ALU.add, ALU.mult), 2)
                dve.wait_ge(sig_ready, n + 1)
                V.tensor_tensor(e_act, e_up, e_sig, ALU.mult).then_inc(act_ready, 1)

            def pair(n, lap, next_lap, next_rnd, first, last_pair):
                if not first:
                    dve.wait_ge(selw_turned, n)
                weigh(n, lap)
                if not last_pair:
                    dve.wait_ge(selw_ready, n + 1)
                    select(next_lap, next_rnd)
                hidden(n, lap)
                if not last_pair:
                    columns_read(n + 1)

            select(0, 0)
            link(V.reciprocal(wrec, wsum))
            V.tensor_scalar(wgt[:, 0], wgt[:, 0], wrec[:, 0:1], None, ALU.mult)
            V.tensor_scalar(wgt[:, 1], wgt[:, 1], wrec[:, 1:2], None, ALU.mult).then_inc(wgt_ready, 1)
            link(V.tensor_reduce(n_max, count, AX.X, ALU.max))
            link(V.tensor_scalar(n_over, n_max, float(CAP), 16.0, ALU.is_gt, ALU.mult))
            for r in (2, 3):
                link(V.tensor_scalar(n_tmp, n_max, float(r * CAP), 16.0, ALU.is_gt, ALU.mult))
                link(V.tensor_tensor(n_over, n_over, n_tmp, ALU.add))
            V.tensor_scalar(last_pair_i, n_over, 15.0, None, ALU.add).then_inc(pairs_ready, 1)
            step0 = steps[0]
            columns_read(0)
            dve.wait_ge(pairs_ready, 1)
            final = dve.value_load(last_pair_i[0:1, :], min_val=15, max_val=63)
            dve.wait_ge(wgt_ready, 1)
            pair(0, 0, 1, 0, True, False)
            with dve.Fori(1, final) as n:
                pair(n, n & 15, (n + 1) & 15, ((n + 1) >> 4) & 3, False, False)
            pair(final, 15, 0, 0, False, True)
            for b in range(4):
                dve.wait_ge(summed, b + 1)
                h = x_sb[:, 2 * b:2 * b + 2, META:ALL]
                V.tensor_tensor(h, h, y_ps[:, 2 * b:2 * b + 2], ALU.add).then_inc(final_ready, 1)


def _chunk_columns():
    q, kv, rq, rv = HEADS * DH, 2 * DH, RH * RDK, RH * RDV
    base = {"q": 0, "k": q, "v": q + kv, "rq": q + 2 * kv}
    base["rk"] = base["rq"] + rq
    base["rv"] = base["rk"] + rq
    base["rg"] = base["rv"] + rv
    base["ga"] = base["rg"] + rv
    base["gr"] = base["ga"] + D
    a = np.arange(DH)

    def columns(kind, i):
        if kind == "q":
            return np.concatenate([i * DH + a, (i + PAIRS) * DH + a])
        return base[kind] + i * P + np.arange(P)
    return columns


def kernel(**inputs):
    import concourse.bacc as bacc
    from concourse.bass_utils import run_bass_kernel_spmd

    a = {k: np.asarray(v) for k, v in inputs.items()}
    h = np.concatenate([a["meta_tokens"], a["x"][0]], 0)
    xT = np.ascontiguousarray(h.T.reshape(KC, P, ALL).transpose(1, 0, 2))
    columns = _chunk_columns()
    w_in = a["w_in"][0]
    rows = np.concatenate([np.concatenate([j * DH + np.arange(DH), (j + PAIRS) * DH + np.arange(DH)])
                           for j in range(PAIRS)])
    full = {"wa": a["w_attn_branch"][0][rows], "wr": a["w_ret_branch"][0], "out": a["w_out"][0]}
    mix_w = np.empty((NU, P, KC, UCOL), np.float32)
    for c, (kind, i) in enumerate(CHUNKS):
        w = full[kind][:, i * P:(i + 1) * P] if kind in full else w_in[:, columns(kind, i)]
        mix_w[c // 2, :, :, (c % 2) * P:(c % 2 + 1) * P] = w.reshape(KC, P, P).transpose(1, 0, 2)
    mix_w = mix_w.reshape(NU, P, KC * UCOL)

    def by_feature(v):
        return v.reshape(KC, P).T

    params = np.concatenate([
        by_feature(a["mix_norm_gain"][0]), by_feature(a["ffn_norm_gain"][0]),
        np.tile(a["q_norm_gain"][0], 2)[:, None], np.tile(a["k_norm_gain"][0], 2)[:, None],
        np.broadcast_to(a["attn_sinks"][0].reshape(2, PAIRS).T.reshape(1, HEADS), (P, HEADS)),
        np.broadcast_to(a["b_router"], (P, EXPERTS)),
        a["w_router"][0].reshape(KC, P, EXPERTS).transpose(1, 0, 2).reshape(P, -1),
        a["b_gate_up"][0].reshape(EXPERTS, 16, P).transpose(2, 0, 1).reshape(P, -1)], 1)
    assert params.shape == (P, N_PARAM)
    arrays = {
        "xT": xT, "mix_w": mix_w, "consts": constants(), "params": np.ascontiguousarray(params),
        "b_down": np.ascontiguousarray(a["b_down"][0]), "w_gate_up": a["w_gate_up"][0], "w_down": a["w_down"][0],
    }
    nc = bacc.Bacc("TRN2", target_bir_lowering=False, num_devices=1)
    args = [nc.dram_tensor(f"in_{k}", v.shape, F32, kind="ExternalInput").ap() for k, v in arrays.items()]
    out = nc.dram_tensor("out", (P, KC, TOK), F32, kind="ExternalOutput").ap()
    build(nc, *args, out)
    r = run_bass_kernel_spmd(nc, [{f"in_{k}": v for k, v in arrays.items()}], core_ids=[0])
    y = np.asarray(r.results[0]["out"])
    return np.ascontiguousarray(y.transpose(2, 1, 0)).reshape(1, TOK, D)
```
